# Optimizing a Trainium2 kernel written in Bass

```python
import jax, jax.numpy as jnp
from jax import lax
import numpy as np

D_MODEL = 1024
BATCH = 1
SEQ = 512
DEPTH = 2

CHUNK = 64
N_PREV_CHUNKS = 8
BAND = (N_PREV_CHUNKS + 1) * CHUNK
N_MEM = 256
MEM_HEADS = 4
MEM_HD = 128
MEM_W = MEM_HEADS * MEM_HD
ATT_HEADS = 16
ATT_HD = 64
ATT_W = ATT_HEADS * ATT_HD
D_RNN = 1280
RG_BLOCKS = 16
RG_BW = D_RNN // RG_BLOCKS
RG_C = 8.0
CONV_A = 4
D_FF = 3072
CONV_FFN = 3
MAX_REL = 256
N_REL = MAX_REL + CHUNK
EPS = 1e-6
N_A = DEPTH // 2
N_B = DEPTH - N_A

kernel_name = 'hybrid_rglru_chunkattn_yoco'

def rmsnorm(x, g):
    xf = x.astype(jnp.float32)
    y = xf * lax.rsqrt(jnp.mean(xf * xf, axis=-1, keepdims=True) + EPS)
    return (y * g.astype(jnp.float32)).astype(x.dtype)

def causal_dwconv(x, w, b):
    width = w.shape[0]
    y = lax.conv_general_dilated(
        x, w[:, None, :].astype(x.dtype), window_strides=(1,),
        padding=[(width - 1, 0)], dimension_numbers=('NWC', 'WIO', 'NWC'),
        feature_group_count=x.shape[-1])
    return y + b.astype(x.dtype)

def block_diag(x, w, b):
    bsz, s, _ = x.shape
    xb = x.reshape(bsz, s, RG_BLOCKS, RG_BW)
    return jnp.einsum('bsnk,nkj->bsnj', xb, w).reshape(bsz, s, D_RNN) + b

def rg_lru(x, w_r, b_r, w_i, b_i, lam):
    r = jax.nn.sigmoid(block_diag(x, w_r, b_r).astype(jnp.float32))
    i = jax.nn.sigmoid(block_diag(x, w_i, b_i).astype(jnp.float32))
    log_a = RG_C * r * jax.nn.log_sigmoid(lam.astype(jnp.float32))
    a = jnp.exp(log_a)
    u = jnp.sqrt(-jnp.expm1(2.0 * log_a)) * i * x.astype(jnp.float32)

    def combine(left, right):
        a_l, b_l = left
        a_r, b_r2 = right
        return a_l * a_r, a_r * b_l + b_r2

    _, h = lax.associative_scan(combine, (a, u), axis=1)
    return h.astype(x.dtype)

def mem_attention(q, mem_n, w_kv, g_q, g_k):
    bsz, s, _ = q.shape
    q = rmsnorm(q.reshape(bsz, s, MEM_HEADS, MEM_HD), g_q)
    kv = mem_n @ w_kv
    k, v = jnp.split(kv, 2, axis=-1)
    k = rmsnorm(k.reshape(bsz, -1, MEM_HEADS, MEM_HD), g_k)
    v = v.reshape(bsz, -1, MEM_HEADS, MEM_HD)
    sc = jnp.einsum('bshd,bmhd->bhsm', q, k).astype(jnp.float32) * (MEM_HD ** -0.5)
    p = jax.nn.softmax(sc, axis=-1).astype(v.dtype)
    return jnp.einsum('bhsm,bmhd->bshd', p, v).reshape(bsz, s, MEM_W)

def chunk_attention(q, k_pad, v_pad, bias_band):
    bsz, s, h, hd = q.shape
    n_chunks = s // CHUNK
    k_pos = jnp.arange(BAND)

    def one_chunk(c):
        qc = lax.dynamic_slice_in_dim(q, c * CHUNK, CHUNK, axis=1)
        kc = lax.dynamic_slice_in_dim(k_pad, c * CHUNK, BAND, axis=1)
        vc = lax.dynamic_slice_in_dim(v_pad, c * CHUNK, BAND, axis=1)
        sc = jnp.einsum('bqhd,bkhd->bhqk', qc, kc).astype(jnp.float32) * (hd ** -0.5) + bias_band
        valid = k_pos >= (N_PREV_CHUNKS - c) * CHUNK
        sc = jnp.where(valid[None, None, None, :], sc, -1e30)
        p = jax.nn.softmax(sc, axis=-1).astype(vc.dtype)
        return jnp.einsum('bhqk,bkhd->bqhd', p, vc)

    out = lax.map(one_chunk, jnp.arange(n_chunks))
    return out.transpose(1, 0, 2, 3, 4).reshape(bsz, s, h * hd)

def conv_ffn(x, w_up, w_dw, b_dw, w_down):
    hid = causal_dwconv(x @ w_up, w_dw, b_dw)
    u, g = jnp.split(hid, 2, axis=-1)
    return (jax.nn.gelu(g) * u) @ w_down

def setup_inputs(seed: int = 0) -> dict:
    key = jax.random.key(seed)
    ks = jax.random.split(key, 32)
    f32 = jnp.float32
    nrm = lambda k, shape, scale: scale * jax.random.normal(k, shape, f32)
    gain = lambda k, shape: 1.0 + 0.05 * jax.random.normal(k, shape, f32)
    u = jax.random.uniform(ks[13], (N_A, D_RNN), f32, minval=0.9, maxval=0.999)
    s_ = u ** (1.0 / RG_C)
    lam_a = jnp.log(s_) - jnp.log1p(-s_)
    return {
        'x': nrm(ks[0], (BATCH, SEQ, D_MODEL), 1.0),
        'mem': nrm(ks[1], (BATCH, N_MEM, D_MODEL), 1.0),
        'g_mix': gain(ks[2], (DEPTH, D_MODEL)),
        'g_mem': gain(ks[3], (DEPTH, D_MODEL)),
        'w_mem_kv': nrm(ks[4], (DEPTH, D_MODEL, 2 * MEM_W), D_MODEL ** -0.5),
        'g_q_mem': gain(ks[5], (DEPTH, MEM_HD)),
        'g_k_mem': gain(ks[6], (DEPTH, MEM_HD)),
        'w_in_a': nrm(ks[7], (N_A, D_MODEL, 2 * D_RNN + MEM_W), D_MODEL ** -0.5),
        'w_conv_a': nrm(ks[8], (N_A, CONV_A, D_RNN), CONV_A ** -0.5),
        'b_conv_a': nrm(ks[9], (N_A, D_RNN), 0.02),
        'w_r_a': nrm(ks[10], (N_A, RG_BLOCKS, RG_BW, RG_BW), RG_BW ** -0.5),
        'b_r_a': nrm(ks[11], (N_A, D_RNN), 0.02),
        'w_i_a': nrm(ks[12], (N_A, RG_BLOCKS, RG_BW, RG_BW), RG_BW ** -0.5),
        'b_i_a': nrm(ks[14], (N_A, D_RNN), 0.02),
        'lam_a': lam_a,
        'w_out_a': nrm(ks[15], (N_A, D_RNN + MEM_W, D_MODEL), (D_RNN + MEM_W) ** -0.5),
        'g_kv': gain(ks[16], (D_MODEL,)),
        'w_kv': nrm(ks[17], (D_MODEL, 2 * ATT_W), D_MODEL ** -0.5),
        'g_k_att': gain(ks[18], (ATT_HD,)),
        'w_in_b': nrm(ks[19], (N_B, D_MODEL, ATT_W + MEM_W), D_MODEL ** -0.5),
        'g_q_att': gain(ks[20], (N_B, ATT_HD)),
        'rel_bias_b': nrm(ks[21], (N_B, ATT_HEADS, N_REL), 0.2),
        'w_out_b': nrm(ks[22], (N_B, ATT_W + MEM_W, D_MODEL), (ATT_W + MEM_W) ** -0.5),
        'g_ffn': gain(ks[23], (DEPTH, D_MODEL)),
        'w_up': nrm(ks[24], (DEPTH, D_MODEL, 2 * D_FF), D_MODEL ** -0.5),
        'w_dw_ffn': nrm(ks[25], (DEPTH, CONV_FFN, 2 * D_FF), CONV_FFN ** -0.5),
        'b_dw_ffn': nrm(ks[26], (DEPTH, 2 * D_FF), 0.02),
        'w_down': nrm(ks[27], (DEPTH, D_FF, D_MODEL), D_FF ** -0.5),
    }

def reference(x, mem, g_mix, g_mem, w_mem_kv, g_q_mem, g_k_mem, w_in_a, w_conv_a, b_conv_a,
              w_r_a, b_r_a, w_i_a, b_i_a, lam_a, w_out_a, g_kv, w_kv, g_k_att, w_in_b,
              g_q_att, rel_bias_b, w_out_b, g_ffn, w_up, w_dw_ffn, b_dw_ffn, w_down):
    bsz, s, _ = x.shape
    rel = jnp.arange(CHUNK)[:, None] + N_PREV_CHUNKS * CHUNK - jnp.arange(BAND)[None, :]
    rel_idx = jnp.clip(rel, -(CHUNK - 1), MAX_REL) + (CHUNK - 1)
    k_pad = None
    v_pad = None
    for l in range(DEPTH):
        h = rmsnorm(x, g_mix[l])
        mem_n = rmsnorm(mem, g_mem[l])
        if l < N_A:
            proj = h @ w_in_a[l]
            xr, yg, qm = jnp.split(proj, [D_RNN, 2 * D_RNN], axis=-1)
            xr = causal_dwconv(xr, w_conv_a[l], b_conv_a[l])
            main = rg_lru(xr, w_r_a[l], b_r_a[l], w_i_a[l], b_i_a[l], lam_a[l]) * jax.nn.gelu(yg)
            w_out = w_out_a[l]
        else:
            j = l - N_A
            if j == 0:
                kv = rmsnorm(x, g_kv) @ w_kv
                k, v = jnp.split(kv, 2, axis=-1)
                k = rmsnorm(k.reshape(bsz, s, ATT_HEADS, ATT_HD), g_k_att)
                v = v.reshape(bsz, s, ATT_HEADS, ATT_HD)
                pad = ((0, 0), (N_PREV_CHUNKS * CHUNK, 0), (0, 0), (0, 0))
                k_pad = jnp.pad(k, pad)
                v_pad = jnp.pad(v, pad)
            proj = h @ w_in_b[j]
            qa, qm = jnp.split(proj, [ATT_W], axis=-1)
            qa = rmsnorm(qa.reshape(bsz, s, ATT_HEADS, ATT_HD), g_q_att[j])
            bias_band = rel_bias_b[j][:, rel_idx].astype(jnp.float32)
            main = chunk_attention(qa, k_pad, v_pad, bias_band)
            w_out = w_out_b[j]
        mo = mem_attention(qm, mem_n, w_mem_kv[l], g_q_mem[l], g_k_mem[l])
        x = x + jnp.concatenate([main, mo], axis=-1) @ w_out
        x = x + conv_ffn(rmsnorm(x, g_ffn[l]), w_up[l], w_dw_ffn[l], b_dw_ffn[l], w_down[l])
    return x


_drawn_inputs = setup_inputs


def setup_inputs(seed=0):
    import zlib

    import numpy as np

    out = dict(_drawn_inputs(seed))
    spreads = {}
    factors = {'g_mem': 8.0,
     'g_q_mem': 8.0,
     'g_k_mem': 8.0,
     'b_r_a': 8.0,
     'b_i_a': 8.0,
     'g_kv': 8.0,
     'g_k_att': 8.0,
     'g_q_att': 8.0,
     'rel_bias_b': 3.473}
    for name, (base, spread) in spreads.items():
        noise = np.random.default_rng([zlib.crc32(name.encode()), seed]).standard_normal(out[name].shape)
        drawn = base * np.exp(spread * noise) if base else spread * noise
        out[name] = __import__('jax').numpy.asarray(drawn.astype(out[name].dtype))
    for name, factor in factors.items():
        out[name] = (out[name] * factor).astype(out[name].dtype)
    return out
```

```python
from contextlib import ExitStack

import concourse.bass as bass
from concourse import mybir

P = 128
F32 = mybir.dt.float32
F32R = mybir.dt.float32r
ALU = mybir.AluOpType
ACT = mybir.ActivationFunctionType
AX = mybir.AxisListType.X

SEQ, D = 512, 1024
KT = D // P
TT = SEQ // P
MEM, MT = 256, 2
MH, MHD = 4, 128
AH, AHD = 16, 64
D_RNN, RT = 1280, 10
RGB = 80
D_FF, FT = 3072, 24
FH = FT // 2
MID = 14
EPS = 1e-6
RG_C = 8.0
OUT0_ORDER = list(range(10, 14)) + list(range(10))
MASKED = -1e30

PHASES = [
    ("memK0", 4, 8), ("memV0", 4, 8), ("qm0", 4, 8), ("xr", RT, 8), ("yg", RT, 8),
    ("gates", RT, 6), ("out0", 16, 7),
    ("up00", 24, 8), ("down00", 16, 6), ("up01", 24, 8), ("down01", 16, 6),
    ("memK1", 4, 8), ("memV1", 4, 8), ("k", 8, 8), ("v", 8, 8), ("q", 8, 8), ("qm1", 4, 8),
    ("out1", 16, 6),
    ("up10", 24, 8), ("down10", 16, 6), ("up11", 24, 8), ("down11", 16, 6),
]
BASE = {}
_at = 0
for _name, _n, _w in PHASES:
    BASE[_name] = _at
    _at += _n
CHUNKS = _at
WIDTH = {name: w for name, _, w in PHASES}
COUNT = {name: n for name, n, _ in PHASES}
RAW = 2
RING = 4
AHEAD = RING - 1

COLS = {}
_at = 0
for _name, _n in [("g_mix0", KT), ("g_mix1", KT), ("g_mem0", KT), ("g_mem1", KT), ("g_kv", KT),
                  ("g_ffn0", KT), ("g_ffn1", KT), ("conv_a", 5 * RT), ("b_r", RT), ("b_i", RT),
                  ("lam", RT), ("g_qm0", 1), ("g_km0", 1), ("g_qm1", 1), ("g_km1", 1),
                  ("g_qa", 1), ("g_ka", 1), ("ffn0", 8 * FT), ("ffn1", 8 * FT)]:
    COLS[_name] = _at
    _at += _n
NCOLS = _at


def gate_k(m):
    first = (P * m) // RGB * RGB
    last = -(-(P * m + P) // RGB) * RGB
    return list(range(first // P, -(-last // P)))


def steps(eng, n, body, peel_first=False, last=None):
    if peel_first:
        body(0)
    with eng.Fori(1 if peel_first else 0, n - (last is not None)) as i:
        body(i)
    if last is not None:
        last(n - 1)


class Tally:

    def __init__(self, eng, sem):
        self.eng, self.sem, self.n, self.i, self.per, self.n0 = eng, sem, 0, None, 0, 0

    def inc(self, ins):
        ins.then_inc(self.sem, 1)
        self.n += 1

    def wait(self):
        self.eng.wait_ge(self.sem, self.n if self.i is None else self.i * self.per + self.n)

    def link(self, ins):
        self.inc(ins)
        self.wait()

    def enter(self, i, per):
        self.i, self.per, self.n0 = i, per, self.n

    def leave(self, times):
        assert self.n - self.n0 == self.per, (self.n - self.n0, self.per)
        self.n, self.i = self.n0 + self.per * times, None


def build(nc, A, out):
    with ExitStack() as ctx:
        def sb(name, shape, dt=F32, stack=ctx, **kw):
            return stack.enter_context(nc.sbuf_tensor(name, shape, dt, **kw))

        def sem(name):
            return ctx.enter_context(nc.semaphore(name))

        xT = sb("xT", [P, KT, SEQ])
        memT = sb("memT", [P, KT, MEM])
        mid_hi = sb("mid_hi", [P, MID, SEQ], F32R)
        mid_lo = sb("mid_lo", [P, MID, SEQ], F32R)
        raw = sb("raw", [P, RAW, 8 * P])
        whi = sb("whi", [P, RING, 8 * P], F32R)
        wlo = sb("wlo", [P, RING, 8 * P], F32R)
        cols = sb("cols", [P, NCOLS])
        ident = sb("ident", [P, P])
        ones = sb("ones", [P, P])
        ssum = sb("ssum", [P, SEQ])
        sq = sb("sq", [P, 2, SEQ])
        tmp = sb("tmp", [P, 2, SEQ])
        diag = sb("diag", [P, TT, P])
        rb = sb("rb", [P, SEQ])
        rb_mem = sb("rb_mem", [P, MEM])
        small = sb("small", [P, 16])
        gs = sb("gs", [P, 3, TT, 8])
        mx = sb("mx", [P, 2, 3, TT])
        nmx = sb("nmx", [P, 2, TT])
        lsc = sb("lsc", [P, 8, RT])
        eps = sb("eps", [P, 1])
        gqs = sb("gqs", [P, 1])
        right = ExitStack()
        hh = sb("hh", [P, KT, SEQ], F32R, right, side="right")
        hl = sb("hl", [P, KT, SEQ], F32R, right, side="right")
        right.close()
        right = ExitStack()
        R = sb("R", [P, 5, SEQ], F32, right, side="right")
        I = sb("I", [P, 5, SEQ], F32, right, side="right")
        Aa = sb("Aa", [P, 5, SEQ], F32, right, side="right")
        right.close()
        right = ExitStack()
        qT = sb("qT", [P, KT, SEQ], F32, right, side="right")
        qmT1 = sb("qmT1", [P, MH, SEQ], F32, right, side="right")
        PTs = sb("PTs", [P, 1280], F32, right, side="right")
        right.close()
        right = ExitStack()
        sb("keep_right", [P, 2 * KT, SEQ], F32, right, side="right")
        ph = ExitStack()
        xc = sb("xc", [P, RT, SEQ], F32, ph)
        kn0 = sb("kn0", [P, TT, SEQ], F32, ph)
        ph2 = ExitStack()
        gy = sb("gy", [P, RT, SEQ], F32, ph2)
        ph2.close()
        qmT0 = sb("qmT0", [P, MH, SEQ], F32, ph)
        kmT0 = sb("kmT0", [P, MH, MEM], F32, ph)
        Vm0 = sb("Vm0", [P, MT, SEQ], F32, ph)
        PTm0 = kn0[:, 0:MT, :]
        Pm0 = kn0[:, MT:TT, :].rearrange("p a b -> p (a b)").rearrange("p (t m) -> p t m", m=MEM)
        ph.close()
        ph = ExitStack()
        uc = sb("uc", [P, 2, SEQ], F32, ph)
        gc = sb("gc", [P, 2, SEQ], F32, ph)
        ph.close()
        ph = ExitStack()
        kT = sb("kT", [P, KT, SEQ], F32, ph)
        V = sb("V", [P, TT, D], F32, ph)
        kmT1 = sb("kmT1", [P, MH, MEM], F32, ph)
        Vm1 = sb("Vm1", [P, MT, SEQ], F32, ph)
        ph2 = ExitStack()
        kn1 = sb("kn1", [P, TT, SEQ], F32, ph2)
        ph2.close()
        Sc = sb("Sc", [P, 2, 1280], F32, ph)
        ph.close()
        PTm1 = kn1[:, 0:MT, :]
        Pm1 = kn1[:, MT:TT, :].rearrange("p a b -> p (a b)").rearrange("p (t m) -> p t m", m=MEM)
        strip = tmp

        bank = [ctx.enter_context(nc.psum_tensor(f"bank{i}", [P, 512], F32)) for i in range(8)]

        raw_in = [sem(f"raw_in{i}") for i in range(RAW)]
        w_hi, w_lo, w_used = sem("w_hi"), sem("w_lo"), sem("w_used")
        x_in, mem_in, const_in, y_out = sem("x_in"), sem("mem_in"), sem("const_in"), sem("y_out")
        strip_in = [sem("strip_in0"), sem("strip_in1")]
        ones_ok, gq_ok, ma_rs = sem("ones_ok"), sem("gq_ok"), sem("ma_rs")
        sq_ready, sq_added = sem("sq_ready"), sem("sq_added")
        st_cols, st_root, st_diag, st_bcast, st_rb = (sem(x) for x in (
            "st_cols", "st_root", "st_diag", "st_bcast", "st_rb"))
        h_tmp, h_hi, h_lo = sem("h_tmp"), sem("h_hi"), sem("h_lo")
        g_sq, g_ss, g_rt, g_kn, g_tp, g_ev, v_ev = (sem(x) for x in (
            "g_sq", "g_ss", "g_rt", "g_kn", "g_tp", "g_ev", "v_ev"))
        xc_0, xc_done, xc_hi, xc_lo = (sem(x) for x in ("xc_0", "xc_done", "xc_hi", "xc_lo"))
        yg_gelu = sem("yg_gelu")
        gt_sig, gt_ix, gt_exp, gt_v, gt_root, gt_main, gt_hi, gt_lo = (sem(x) for x in (
            "gt_sig", "gt_ix", "gt_exp", "gt_v", "gt_root", "gt_main", "gt_hi", "gt_lo"))
        lam_e = sem("lam_e")
        lam_c = sem("lam_c")
        ma_s, ma_nm, ma_e, ma_p, ma_t, ma_pt, ma_pv, ma_hi, ma_lo = (sem("ma_" + x) for x in (
            "s", "nm", "e", "p", "t", "pt", "pv", "hi", "lo"))
        ca_s, ca_add, ca_nm, ca_e, ca_rs, ca_p, ca_t, ca_pta, ca_ptd, ca_pv, ca_hi, ca_lo = (
            sem("ca_" + x) for x in (
                "s", "add", "nm", "e", "rs", "p", "t", "pta", "ptd", "pv", "hi", "lo"))
        up_first, up_conv, up_gelu, up_hid, up_hi, up_lo = (sem("up_" + x) for x in (
            "first", "conv", "gelu", "hid", "hi", "lo"))
        o_add = sem("o_add")
        dve_own = sem("dve_own")

        H = {n: i for i, n in enumerate(["mem0", "mix0", "ffn0", "mem1", "kv", "mix1", "ffn1"])}
        ST = {n: i for i, n in enumerate(["mem", "mix0", "ffn0", "kv", "ffn1"])}
        GROUPS = [("memK0", "mem0", MT, MHD), ("memV0", "mem0", MT, 0), ("qm0", "mix0", TT, MHD),
                  ("memK1", "mem1", MT, MHD), ("memV1", "mem1", MT, 0),
                  ("k", "kv", TT, AHD), ("k'", "kv", TT, AHD), ("v", "kv", TT, 0), ("v'", "kv", TT, 0),
                  ("q", "mix1", TT, AHD), ("q'", "mix1", TT, AHD), ("qm1", "mix1", TT, MHD)]
        GI = {g[0]: i for i, g in enumerate(GROUPS)}
        GT0, NB0, VB0, NI = [], [], [], []
        a = b = c = d = 0
        for _, _, t, hd in GROUPS:
            GT0.append(a); NB0.append(b); VB0.append(c); NI.append(d)
            a += t
            if hd:
                b += t
                d += 1
            else:
                c += t
        NLAST = {}
        prev = None
        for i, g in enumerate(GROUPS):
            NLAST[i] = prev
            if g[3]:
                prev = i

        def gset(i):
            return bank[4 * (i % 2):4 * (i % 2) + 4]

        def chunk_of(name, j=0):
            second = name.endswith("'")
            return BASE[name.rstrip("'")] + 4 * second + j

        memh_hi = mid_hi[:, 10:14, :].rearrange("p a b -> p (a b)").rearrange("p (k m) -> p k m", m=MEM)
        memh_lo = mid_lo[:, 10:14, :].rearrange("p a b -> p (a b)").rearrange("p (k m) -> p k m", m=MEM)
        HDST = {"mem0": (memh_hi, memh_lo), "mem1": (memh_hi, memh_lo),
                "mix0": (hh, hl), "ffn0": (hh, hl), "kv": (hh, hl), "ffn1": (hh, hl),
                "mix1": (mid_hi, mid_lo)}

        def col(name, j=0):
            return cols[:, COLS[name] + j:COLS[name] + j + 1]

        NORM_TILES = NB0[-1] + TT

        def col_n(name, n):
            return cols[:, COLS[name]:COLS[name] + n]

        def conv_high(act, i):
            act.wait_ge(xc_done, i + 1)
            act.activation(mid_hi[:, i, :], xc[:, i, :], ACT.Copy).then_inc(xc_hi, 1)

        def ca_high(act, p):
            act.wait_ge(ca_pv, 2 * p + 2)
            act.activation(mid_hi[:, p, :], bank[3][:], ACT.Copy).then_inc(ca_hi, 1)

        def gate_high(act, m):
            act.wait_ge(gt_main, m + 1)
            act.activation(mid_hi[:, m, :], xc[:, m, :], ACT.Copy).then_inc(gt_hi, 1)

        def gate_low(dve, m):
            dve.wait_ge(gt_hi, m + 1)
            dve.tensor_tensor(mid_lo[:, m, :], xc[:, m, :], mid_hi[:, m, :].bitcast(F32), ALU.subtract)\
                .then_inc(gt_lo, 1)

        OUTS = ["out0", "down00", "down01", "out1", "down10", "down11"]
        OI = {n: KT * i for i, n in enumerate(OUTS)}
        UPS = ["up00", "up01", "up10", "up11"]
        UI = {n: i for i, n in enumerate(UPS)}
        SQ = {"mem": 0, "mix0": KT, "out0": 2 * KT, "down01": 3 * KT, "out1": 4 * KT}
        STAT_OF = {"out0": "ffn0", "down01": "kv", "out1": "ffn1"}

        block = ctx.enter_context(nc.Block())

        @block.sync
        def _(sp):
            sp.dma_start(memT[:], A["memT"]).then_inc(mem_in, 16)
            for c in range(RAW):
                sp.dma_start(raw[:, c], A["w_memK0"][c]).then_inc(raw_in[c], 16)
            sp.dma_start(cols[:], A["cols"]).then_inc(const_in, 16)
            sp.dma_start(ident[:], A["ident"]).then_inc(const_in, 16)
            for c in range(RAW, COUNT["memK0"]):
                sp.wait_ge(w_lo, c - RAW + 1)
                sp.dma_start(raw[:, c % RAW], A["w_memK0"][c]).then_inc(raw_in[c % RAW], 16)
            for k in range(0, KT, 4):
                sp.dma_start(xT[:, k:k + 4], A["xT"][:, k:k + 4]).then_inc(x_in, 16)
            def load(name, first, n):
                with sp.Fori(first // RAW, n // RAW) as i:
                    for j in range(RAW):
                        c = BASE[name] + j
                        sp.wait_ge(w_lo, RAW * i + (c - RAW + 1))
                        sp.dma_start(raw[:, c % RAW, 0:WIDTH[name] * P], A["w_" + name][RAW * i + j])\
                            .then_inc(raw_in[c % RAW], 16)

            for name, n, _ in PHASES[1:]:
                if name != "out1":
                    load(name, 0, n)
                    continue
                load(name, 0, RING)
                sp.wait_ge(h_lo, KT * (H["mix1"] + 1))
                for a in range(AH):
                    if a >= 2:
                        sp.wait_ge(ca_add, TT * (a - 1))
                    sp.dma_start(strip[:, a % 2], A["strips"][a]).then_inc(strip_in[a % 2], 16)
                load(name, RING, n)
            for k in range(KT):
                sp.wait_ge(o_add, OI["down11"] + k + 1)
                sp.dma_start(out[:, k], xT[:, k]).then_inc(y_out, 16)
            sp.wait_ge(y_out, 16 * KT)

        @block.gpsimd
        def _(pool):
            def split_lo(i, j):
                pool.wait_ge(w_hi, RING * i + j + 1)
                nc.gpsimd.tensor_tensor(wlo[:, j], raw[:, j % RAW], whi[:, j].bitcast(F32), ALU.subtract)\
                    .then_inc(w_lo, 1)
            with pool.Fori(0, CHUNKS // RING) as i:
                for j in range(RING):
                    split_lo(i, j)
            for j in range(CHUNKS % RING):
                split_lo(CHUNKS // RING, j)

        @block.tensor
        def _(pe):
            def pass3(o, w_h, w_l, x_h, x_l, start, stop):
                nc.tensor.matmul(o, w_h, x_h, start=start, stop=False)
                nc.tensor.matmul(o, w_h, x_l, start=False, stop=False)
                return nc.tensor.matmul(o, w_l, x_h, start=False, stop=stop)

            def colsum(inst, n):
                pe.wait_ge(sq_added, KT * (ST[inst] + 1))
                for t in range(n // P):
                    mm = nc.tensor.matmul(bank[6][:, t:t + 1], ssum[:, t * P:(t + 1) * P], ones[:, 0:1],
                                          start=t == 0, stop=True, skip_group_check=True)
                mm.then_inc(st_cols, 1)

            def bcast(inst, n):
                pe.wait_ge(st_diag, ST[inst] + 1)
                nc.tensor.matmul(bank[7][:, 0:n], ones[:], diag[:, 0:n // P, :], start=True, stop=True)\
                    .then_inc(st_bcast, 1)

            def free_set(g):
                if g >= 2:
                    if GROUPS[g - 2][3]:
                        pe.wait_ge(g_ev, NB0[g - 2] + GROUPS[g - 2][2])
                    else:
                        pe.wait_ge(v_ev, VB0[g - 2] + GROUPS[g - 2][2])
                if g == GI["memK1"]:
                    pe.wait_ge(o_add, OI["down01"] + KT)
                if g == GI["memV1"]:
                    pe.wait_ge(up_conv, 2 * FH * 2)

            def group(g, between=None):
                name, inp, T, hd = GROUPS[g]
                dh, dl = HDST[inp]
                free_set(g)
                for j in range(4):
                    c = chunk_of(name, j)
                    pe.wait_ge(w_lo, c + 1)
                    for q in range(2):
                        k = 2 * j + q
                        pe.wait_ge(h_lo, KT * H[inp] + k + 1)
                        for t in range(T):
                            mm = pass3(gset(g)[t][:], dh[:, k, t * P:(t + 1) * P], dl[:, k, t * P:(t + 1) * P],
                                       whi[:, c % RING, q * 512:(q + 1) * 512],
                                       wlo[:, c % RING, q * 512:(q + 1) * 512], k == 0, k == KT - 1)
                    mm.then_inc(w_used, 1)
                    if j == 1 and between is not None:
                        between()

            def group_transposes(g):
                name, _, T, hd = GROUPS[g]
                kn = kn0 if g < GI["memK1"] else kn1
                for t in range(T):
                    if t == 0:
                        pe.wait_ge(g_kn, NB0[g] + T)
                    for f in range(4):
                        mm = nc.tensor.transpose(gset(g)[t][:, f * P:(f + 1) * P],
                                                 kn[:, t, f * P:(f + 1) * P], ident[:])
                    mm.then_inc(g_tp, 1)

            def fm_tile(o, c, slot, inp, nk, free):
                dh, dl = HDST[inp]
                pe.wait_ge(w_lo, c + 1)
                if free is not None:
                    pe.wait_ge(*free)
                for k in range(nk):
                    pe.wait_ge(h_lo, KT * H[inp] + k + 1) if free_first(inp) else None
                    mm = pass3(o, whi[:, slot, k * P:(k + 1) * P], wlo[:, slot, k * P:(k + 1) * P],
                               dh[:, k, :], dl[:, k, :], k == 0, k == nk - 1)
                mm.then_inc(w_used, 1)

            seen = set()

            def free_first(inp):
                return inp not in seen

            def ma_scores(L, h):
                u = MH * L + h
                qm, km = (qmT0, kmT0) if L == 0 else (qmT1, kmT1)
                if h == 0:
                    pe.wait_ge(g_ev, NB0[GI["qm%d" % L]] + TT)
                for half in range(2):
                    if u > 0:
                        pe.wait_ge(ma_nm, u)
                        pe.wait_ge(ma_e, TT * (u - 1) + 2 * half + 2)
                    for t in range(2):
                        tt = 2 * half + t
                        mm = nc.tensor.matmul(bank[6 + half][:, t * MEM:(t + 1) * MEM],
                                              qm[:, h, tt * P:(tt + 1) * P], km[:, h, :],
                                              start=t == 0, stop=True, skip_group_check=True)
                    mm.then_inc(ma_s, 1)

            def ma_transposes(L, h):
                u = MH * L + h
                Pm = Pm0 if L == 0 else Pm1
                pe.wait_ge(ma_p, u + 1)
                if u > 0:
                    pe.wait_ge(ma_pt, u)
                for m in range(MT):
                    for t in range(TT):
                        mm = nc.tensor.transpose(bank[m][:, t * P:(t + 1) * P],
                                                 Pm[:, t, m * P:(m + 1) * P], ident[:])
                mm.then_inc(ma_t, 1)

            def ma_values(L, h):
                u = MH * L + h
                Vm, PTm = (Vm0, PTm0) if L == 0 else (Vm1, PTm1)
                pe.wait_ge(ma_pt, u + 1)
                pe.wait_ge(v_ev, VB0[GI["memV%d" % L]] + MT)
                if h > 1:
                    pe.wait_ge(ma_lo, u - 1)
                for m in range(MT):
                    mm = nc.tensor.matmul(bank[2 + h % 2][:], Vm[:, m, h * MHD:(h + 1) * MHD],
                                          PTm[:, m, :], start=m == 0, stop=m == MT - 1)
                mm.then_inc(ma_pv, 1)

            def ca_scores(a):
                p0 = AHD * (a % 2)
                for t in range(TT):
                    if a >= 1:
                        pe.wait_ge(ca_add, TT * (a - 1) + t + 1)
                    n = P * (t + 1)
                    nc.tensor.matmul(bank[4 + t][:, 0:n], qT[p0:p0 + AHD, a // 2, t * P:(t + 1) * P],
                                     kT[p0:p0 + AHD, a // 2, 0:n], start=True, stop=True).then_inc(ca_s, 1)

            PT_BANK = [(0, 0), (1, 0), (2, 0), (1, 384)]
            PT_AT = [0, 512, 1024, 896]

            def ca_transposes(a):
                pe.wait_ge(ca_p, a + 1)
                if a >= 1:
                    pe.wait_ge(ca_pta, a)
                    pe.wait_ge(ca_ptd, 2 * a)
                at = 0
                for t in range(TT):
                    for kt in range(t + 1):
                        b, o = PT_BANK[kt]
                        o += (t - kt) * P
                        mm = nc.tensor.transpose(bank[b][:, o:o + P], Sc[:, a % 2, at + kt * P:at + (kt + 1) * P],
                                                 ident[:])
                    at += P * (t + 1)
                mm.then_inc(ca_t, 1)

            def ca_values(a):
                pe.wait_ge(ca_pta, a + 1)
                pe.wait_ge(ca_ptd, 2 * a + 2)
                if a % 2 == 0 and a > 0:
                    pe.wait_ge(ca_lo, a // 2)
                p0 = AHD * (a % 2)
                for kt in range(TT):
                    n = SEQ - kt * P
                    mm = nc.tensor.matmul(bank[3][p0:p0 + AHD, kt * P:SEQ], V[:, kt, a * AHD:(a + 1) * AHD],
                                          PTs[:, PT_AT[kt]:PT_AT[kt] + n], start=kt == 0, stop=kt == TT - 1)
                mm.then_inc(ca_pv, 1)

            def out_proj(name, order, ready):
                nk = len(order)

                def body(i):
                    for m in range(2):
                        n = 0
                        for half in range(2):
                            c = BASE[name] + 2 * m + half
                            pe.wait_ge(w_lo, RING * i + c + 1)
                            if half == 0 and not (name == "out0" and isinstance(i, int)):
                                pe.wait_ge(o_add, 2 * i + (OI[name] + m - 1))
                            for q in range(nk // 2):
                                if m == 0 and n in ready:
                                    for w in ready[n]:
                                        pe.wait_ge(*w)
                                k = order[n]
                                mm = pass3(bank[4 + m][:], whi[:, c % RING, q * P:(q + 1) * P],
                                           wlo[:, c % RING, q * P:(q + 1) * P], mid_hi[:, k, :], mid_lo[:, k, :],
                                           n == 0, n == nk - 1)
                                n += 1
                            mm.then_inc(w_used, 1)
                steps(pe, KT // 2, body, name == "out0")

            def ffn_up(name):
                dh, dl = HDST["ffn" + name[2]]
                U = UI[name]
                inp = KT * H["ffn" + name[2]]
                def body(i):
                    for p in range(2):
                        for s in range(2):
                            c = BASE[name] + 2 * p + s
                            pe.wait_ge(w_lo, RING * i + c + 1)
                            if not (name == "up00" and isinstance(i, int)):
                                pe.wait_ge(up_conv, RING * i + (2 * FH * U + 2 * p + s - 3))
                            for k in range(KT):
                                if p == 0 and s == 0:
                                    pe.wait_ge(h_lo, inp + k + 1)
                                mm = pass3(bank[2 * s + p][:], whi[:, c % RING, k * P:(k + 1) * P],
                                           wlo[:, c % RING, k * P:(k + 1) * P], dh[:, k, :], dl[:, k, :],
                                           k == 0, k == KT - 1)
                            mm.then_inc(w_used, 1)
                steps(pe, FH // 2, body, name == "up00")

            def ffn_down(name):
                U = UI["up" + name[4:]]
                out_proj(name, list(range(FH)),
                         {0: [(up_lo, FH * U + FH - 1)], FH - 1: [(up_lo, FH * U + FH)]})

            pe.wait_ge(const_in, 32)
            pe.wait_ge(ones_ok, 1)
            colsum("mem", MEM)
            bcast("mem", MEM)
            colsum("mix0", SEQ)
            bcast("mix0", SEQ)
            group(GI["memK0"])
            group(GI["memV0"], lambda: group_transposes(GI["memK0"]))
            group(GI["qm0"])
            for i in range(RT):
                c = BASE["xr"] + i
                if i == 0:
                    pe.wait_ge(v_ev, MT)
                fm_tile(bank[4 + i % 2][:], c, c % RING, "mix0", KT,
                        (xc_done, i - 1) if i >= 2 else None)
                seen.add("mix0")
                if i == 1:
                    group_transposes(GI["qm0"])
                if 4 <= i < 4 + MH:
                    ma_values(0, i - 4)
                if 3 <= i < 3 + MH:
                    ma_transposes(0, i - 3)
                if 2 <= i < 2 + MH:
                    ma_scores(0, i - 2)
            for i in range(RT):
                c = BASE["yg"] + i
                fm_tile(bank[4 + i % 2][:], c, c % RING, "mix0", KT,
                        (xc_done, RT - 1 + i) if i < 2 else (yg_gelu, i - 1))
            pe.wait_ge(ma_lo, MH)
            pe.wait_ge(xc_lo, RT)
            for i in range(RT):
                c = BASE["gates"] + i
                pe.wait_ge(w_lo, c + 1)
                if i == 0:
                    pe.wait_ge(yg_gelu, RT)
                if i >= 4:
                    pe.wait_ge(gt_sig, i - 3)
                ks = gate_k(i)
                for gate in range(2):
                    for n, k in enumerate(ks):
                        q = gate * len(ks) + n
                        mm = pass3(bank[4 * gate + i % 4][:], whi[:, c % RING, q * P:(q + 1) * P],
                                   wlo[:, c % RING, q * P:(q + 1) * P], mid_hi[:, k, :], mid_lo[:, k, :],
                                   n == 0, n == len(ks) - 1)
                mm.then_inc(w_used, 1)
            pe.wait_ge(gt_sig, RT)
            out_proj("out0", OUT0_ORDER, {MH + k: [(gt_lo, k + 1)] for k in range(RT)})
            colsum("ffn0", SEQ)
            bcast("ffn0", SEQ)
            ffn_up("up00")
            ffn_down("down00")
            ffn_up("up01")
            ffn_down("down01")
            group(GI["memK1"])
            colsum("kv", SEQ)
            bcast("kv", SEQ)
            group(GI["memV1"], lambda: group_transposes(GI["memK1"]))
            group(GI["k"])
            group(GI["k'"], lambda: group_transposes(GI["k"]))
            group(GI["v"], lambda: group_transposes(GI["k'"]))
            group(GI["v'"])
            group(GI["q"])
            group(GI["q'"], lambda: group_transposes(GI["q"]))
            group(GI["qm1"], lambda: group_transposes(GI["q'"]))
            group_transposes(GI["qm1"])
            for i in range(MH + 2):
                if i >= 2:
                    ma_values(1, i - 2)
                if 1 <= i <= MH:
                    ma_transposes(1, i - 1)
                if i < MH:
                    ma_scores(1, i)
            pe.wait_ge(ma_lo, 2 * MH)
            pe.wait_ge(v_ev, VB0[GI["v'"]] + TT)
            for a in range(AH + 2):
                if a < AH:
                    ca_scores(a)
                if 1 <= a <= AH:
                    ca_transposes(a - 1)
                if a >= 2:
                    ca_values(a - 2)
            out_proj("out1", list(range(FH)), {0: [(ma_lo, 2 * MH), (ca_lo, AH // 2), (ca_add, TT * AH)]})
            colsum("ffn1", SEQ)
            bcast("ffn1", SEQ)
            ffn_up("up10")
            ffn_down("down10")
            ffn_up("up11")
            ffn_down("down11")

        @block.scalar
        def _(act):
            def split_hi(c, i=0, per=0):
                n = c + AHEAD
                act.wait_ge(raw_in[n % RAW], (16 * per // RAW) * i + 16 * (n // RAW + 1))
                if n >= RING:
                    act.wait_ge(w_used, per * i + (n - RING + 1))
                act.activation(whi[:, n % RING], raw[:, n % RAW], ACT.Copy).then_inc(w_hi, 1)

            def square(base, src, k, n, i=0, per=0):
                if base + k - 1 > 0:
                    act.wait_ge(sq_added, per * i + (base + k - 1))
                act.activation(sq[:, k % 2, 0:n], src, ACT.Square).then_inc(sq_ready, 1)

            def stat(inst, n):
                S = ST[inst]
                act.wait_ge(st_cols, S + 1)
                if S > 0:
                    act.wait_ge(st_diag, S)
                act.activation(small[:, 0:n // P], bank[6][:, 0:n // P], ACT.Sqrt, bias=eps[:],
                               scale=1.0 / D).then_inc(st_root, 1)
                act.wait_ge(st_bcast, S + 1)
                dst = rb_mem if inst == "mem" else rb
                if S > 1:
                    act.wait_ge(h_tmp, {"ffn0": 2, "kv": 4, "ffn1": 6}[inst] * KT)
                act.activation(dst[:, 0:n], bank[7][:, 0:n], ACT.Copy).then_inc(st_rb, 1)

            def norm_hi(inst):
                n = MEM if inst.startswith("mem") else SEQ
                dh, _ = HDST[inst]
                for k in range(KT):
                    act.wait_ge(h_tmp, KT * H[inst] + k + 1)
                    act.activation(dh[:, k, 0:n], tmp[:, k % 2, 0:n], ACT.Copy).then_inc(h_hi, 1)

            def group_squares(g):
                name, _, T, hd = GROUPS[g]
                if not hd:
                    return
                act.wait_ge(w_used, chunk_of(name, 3) + 1)
                if g < GI["memK1"]:
                    act.wait_ge(sq_added, 2 * KT)
                else:
                    act.wait_ge(sq_added, (3 if name == "memK1" else 4) * KT)
                for t in range(T):
                    if NB0[g] + t >= 2:
                        act.wait_ge(g_ss, NB0[g] + t - 1)
                    act.activation(sq[:, t % 2], gset(g)[t][:], ACT.Square).then_inc(g_sq, 1)
                act.wait_ge(g_ss, NB0[g] + T)
                if NB0[g] > 0:
                    act.wait_ge(g_kn, NB0[g])
                nh = 512 // hd
                act.activation(gs[:, 1, 0:T, 0:nh], gs[:, 0, 0:T, 0:nh], ACT.Sqrt, bias=eps[:],
                               scale=1.0 / hd).then_inc(g_rt, 1)

            def group_evac(g):
                name, _, T, hd = GROUPS[g]
                dst, f0, gain = {
                    "memK0": (kmT0, 0, col("g_km0")), "qm0": (qmT0, 0, col("g_qm0")),
                    "memK1": (kmT1, 0, col("g_km1")), "qm1": (qmT1, 0, col("g_qm1")),
                    "k": (kT, 0, col("g_ka")), "k'": (kT, 4, col("g_ka")),
                    "q": (qT, 0, gqs[:]), "q'": (qT, 4, gqs[:])}[name]
                for t in range(T):
                    act.wait_ge(g_tp, NB0[g] + t + 1)
                    act.activation(dst[:, f0:f0 + 4, t * P:(t + 1) * P],
                                   gset(g)[t][:].rearrange("p (f t) -> p f t", f=4), ACT.Copy,
                                   scale=gain).then_inc(g_ev, 1)

            def group_steps(name, after, evac):
                for j in range(4):
                    split_hi(chunk_of(name, j))
                    if j == 0 and after is not None:
                        group_squares(after)
                    if j == 2 and evac is not None:
                        group_evac(evac)

            def ma_exps(L, h):
                u = MH * L + h
                Pm = Pm0 if L == 0 else Pm1
                act.wait_ge(ma_nm, u + 1)
                if u > 0:
                    act.wait_ge(ma_t, u)
                    act.wait_ge(ma_rs, u)
                for t in range(TT):
                    act.activation(Pm[:, t, :], bank[6 + t // 2][:, (t % 2) * MEM:(t % 2 + 1) * MEM], ACT.Exp,
                                   bias=nmx[:, 0, t:t + 1], scale=MHD ** -0.5,
                                   accum_out=mx[:, 0, 1, t:t + 1]).then_inc(ma_e, 1)

            def ma_high(L, h):
                u = MH * L + h
                act.wait_ge(ma_pv, u + 1)
                act.activation(mid_hi[:, (RT, KT)[L] + h, :], bank[2 + h % 2][:], ACT.Copy).then_inc(ma_hi, 1)

            def out_steps(name, stat_base, last=False):
                def body(i, stop=RING):
                    for m in range(2):
                        for half in range(2):
                            if 2 * m + half < stop:
                                split_hi(BASE[name] + 2 * m + half, i, RING)
                        if stat_base is not None:
                            act.wait_ge(o_add, 2 * i + (OI[name] + m + 1))
                            square(stat_base, xT[:, 2 * i + m, :], m, SEQ, i, 2)
                steps(act, KT // 2, body, False, (lambda i: body(i, RING - AHEAD)) if last else None)

            def up_steps(name):
                U = UI[name]
                L = name[2]
                q0 = FH * (U % 2)
                def body(i):
                    for p in range(2):
                        n = FH * U + p
                        for s, acc in ((0, uc), (1, gc)):
                            split_hi(BASE[name] + 2 * p + s, i, RING)
                            act.wait_ge(w_used, RING * i + (BASE[name] + 2 * p + s + 1))
                            if not (name == "up00" and isinstance(i, int)):
                                act.wait_ge(up_lo, 2 * i + (n - 1))
                            f = COLS["ffn" + L] + 8 * (q0 + p) + 4 * s
                            act.activation(acc[:, p, :], bank[2 * s + p][:], ACT.Identity,
                                           bias=cols[:, bass.ds(16 * i + (f + 3), 1)],
                                           scale=cols[:, bass.ds(16 * i + f, 1)]).then_inc(up_first, 1)
                        act.wait_ge(up_conv, RING * i + (2 * n + 2))
                        act.activation(gc[:, p, :], gc[:, p, :], ACT.Gelu_apprx_tanh).then_inc(up_gelu, 1)
                        act.wait_ge(up_hid, 2 * i + (n + 1))
                        act.activation(mid_hi[:, 2 * i + p, :], uc[:, p, :], ACT.Copy).then_inc(up_hi, 1)
                steps(act, FH // 2, body, name == "up00")

            act.wait_ge(ones_ok, 1)
            act.wait_ge(mem_in, 16)
            for k in range(KT):
                square(0, memT[:, k, :], k, MEM)
            for c in range(AHEAD):
                split_hi(c - AHEAD)
            act.wait_ge(x_in, 32)
            stat("mem", MEM)
            for k in range(KT):
                square(KT, xT[:, k, :], k, SEQ)
            norm_hi("mem0")
            stat("mix0", SEQ)
            norm_hi("mix0")
            act.wait_ge(const_in, 32)
            act.activation(lsc[:, 0, :], col_n("lam", RT), ACT.Abs).then_inc(lam_e, 1)
            act.wait_ge(lam_e, 1)
            act.activation(lsc[:, 1, :], lsc[:, 0, :], ACT.Exp, scale=-1.0).then_inc(lam_e, 1)
            group_steps("memK0", None, None)
            group_steps("memV0", GI["memK0"], GI["memK0"])
            group_steps("qm0", None, None)
            for i in range(RT):
                c = BASE["xr"] + i
                split_hi(c)
                if i == 0:
                    group_squares(GI["qm0"])
                if i == 2:
                    group_evac(GI["qm0"])
                act.wait_ge(w_used, c + 1)
                act.activation(xc[:, i, :], bank[4 + i % 2][:], ACT.Identity, bias=col("conv_a", 5 * i + 4),
                               scale=col("conv_a", 5 * i + 3)).then_inc(xc_0, 1)
                if i >= 1:
                    conv_high(act, i - 1)
                if 4 <= i < 4 + MH:
                    ma_high(0, i - 4)
                if 2 <= i < 2 + MH:
                    ma_exps(0, i - 2)
            conv_high(act, RT - 1)
            for i in range(RT):
                c = BASE["yg"] + i
                split_hi(c)
                act.wait_ge(w_used, c + 1)
                act.activation(gy[:, i, :], bank[4 + i % 2][:], ACT.Gelu_apprx_tanh).then_inc(yg_gelu, 1)
            for i in range(RT):
                j, half = i % 5, i // 5
                split_hi(BASE["gates"] + i)
                act.wait_ge(w_used, BASE["gates"] + i + 1)
                if half == 1:
                    act.wait_ge(gt_main, j + 1)
                act.activation(R[:, j, :], bank[i % 4][:], ACT.Sigmoid, bias=col("b_r", i))
                act.activation(I[:, j, :], bank[4 + i % 4][:], ACT.Sigmoid, bias=col("b_i", i))\
                    .then_inc(gt_sig, 1)
                if j == 4:
                    act.wait_ge(lam_c, 1)
                    act.wait_ge(gt_sig, i + 1)
                    for t in range(5):
                        m = 5 * half + t
                        act.activation(Aa[:, t, :], R[:, t, :], ACT.Exp, scale=lsc[:, 7, m:m + 1])\
                            .then_inc(gt_exp, 1)
                        act.wait_ge(gt_exp, 2 * m + 1)
                        act.activation(R[:, t, :], R[:, t, :], ACT.Tanh, scale=lsc[:, 7, m:m + 1])\
                            .then_inc(gt_exp, 1)
                    if half:
                        for m in range(5):
                            gate_high(act, m)
                    for t in range(5):
                        m = 5 * half + t
                        act.wait_ge(gt_v, m + 1)
                        act.activation(R[:, t, :], R[:, t, :], ACT.Sqrt, scale=-1.0).then_inc(gt_root, 1)
                    if half:
                        for m in range(5, RT):
                            gate_high(act, m)
            out_steps("out0", SQ["out0"])
            stat("ffn0", SEQ)
            norm_hi("ffn0")
            up_steps("up00")
            out_steps("down00", None)
            up_steps("up01")
            out_steps("down01", SQ["down01"])
            norm_hi("mem1")
            split_hi(chunk_of("memK1", 0))
            stat("kv", SEQ)
            norm_hi("kv")
            norm_hi("mix1")
            for j in range(1, 4):
                split_hi(chunk_of("memK1", j))
            group_steps("memV1", GI["memK1"], GI["memK1"])
            group_steps("k", None, None)
            group_steps("k'", GI["k"], GI["k"])
            group_steps("v", GI["k'"], GI["k'"])
            group_steps("v'", None, None)
            group_steps("q", None, None)
            group_steps("q'", GI["q"], GI["q"])
            group_steps("qm1", GI["q'"], GI["q'"])
            group_squares(GI["qm1"])
            group_evac(GI["qm1"])
            for i in range(MH + 2):
                if i >= 2:
                    ma_high(1, i - 2)
                if i < MH:
                    ma_exps(1, i)
            for a in range(AH + 2):
                if a >= 2:
                    act.wait_ge(ca_t, a - 1)
                    if a >= 3:
                        act.wait_ge(ca_pv, a - 2)
                    act.activation(PTs[:, 0:512], bank[0][:], ACT.Copy).then_inc(ca_pta, 1)
                if a >= 4 and a % 2 == 0:
                    ca_high(act, a // 2 - 2)
                if a < AH:
                    act.wait_ge(ca_nm, a + 1)
                    at = 0
                    for t in range(TT):
                        n = P * (t + 1)
                        act.activation(Sc[:, a % 2, at:at + n], Sc[:, a % 2, at:at + n], ACT.Exp,
                                       bias=nmx[:, a % 2, t:t + 1],
                                       accum_out=mx[:, a % 2, 1, t:t + 1]).then_inc(ca_e, 1)
                        at += n
            ca_high(act, AH // 2 - 1)
            out_steps("out1", SQ["out1"])
            stat("ffn1", SEQ)
            norm_hi("ffn1")
            up_steps("up10")
            out_steps("down10", None)
            up_steps("up11")
            out_steps("down11", None, last=True)

        @block.vector
        def _(dve):
            own = Tally(dve, dve_own)

            def add_square(base, k, n, i=0, per=0):
                dve.wait_ge(sq_ready, per * i + (base + k + 1))
                if base + k > 0:
                    dve.wait_ge(sq_added, per * i + (base + k))
                dve.tensor_tensor(ssum[:, 0:n], ssum[:, 0:n], sq[:, k % 2, 0:n], ALU.add).then_inc(sq_added, 1)

            def clear_sum(inst):
                if ST[inst] > 0:
                    dve.wait_ge(st_cols, ST[inst])
                own.link(dve.memset(ssum[:], 0.0))

            def stat(inst, n):
                S = ST[inst]
                dve.wait_ge(st_root, S + 1)
                own.link(dve.reciprocal(small[:, 4:4 + n // P], small[:, 0:n // P]))
                if S > 0:
                    dve.wait_ge(st_bcast, S)
                for t in range(n // P):
                    ins = dve.tensor_scalar(diag[:, t, :], ident[:], small[:, 4 + t:5 + t], None, ALU.mult)
                ins.then_inc(st_diag, 1)

            def norm(inst, gname, stat_of):
                mem = inst.startswith("mem")
                n = MEM if mem else SEQ
                src, r = (memT, rb_mem) if mem else (xT, rb)
                dh, dl = HDST[inst]
                dve.wait_ge(st_rb, ST[stat_of] + 1)
                base = KT * H[inst]

                def low(k):
                    dve.wait_ge(h_hi, base + k + 1)
                    dve.wait_ge(h_tmp, base + k + 1)
                    dve.tensor_tensor(dl[:, k, 0:n], tmp[:, k % 2, 0:n], dh[:, k, 0:n].bitcast(F32),
                                      ALU.subtract).then_inc(h_lo, 1)
                for k in range(KT):
                    if base + k >= 2:
                        dve.wait_ge(h_lo, base + k - 1)
                    dve.scalar_tensor_tensor(out=tmp[:, k % 2, 0:n], in0=src[:, k, :], scalar=col(gname, k),
                                             in1=r[:, 0:n], op0=ALU.mult, op1=ALU.mult).then_inc(h_tmp, 1)
                    if k >= 1:
                        low(k - 1)
                low(KT - 1)

            def group_norm(g):
                name, _, T, hd = GROUPS[g]
                nh = 512 // hd
                kn = kn0 if g < GI["memK1"] else kn1
                for t in range(T):
                    dve.wait_ge(g_sq, NB0[g] + t + 1)
                    if NI[g] > 0:
                        dve.wait_ge(g_rt, NI[g])
                    dve.tensor_reduce(gs[:, 0, t, 0:nh], sq[:, t % 2].rearrange("p (h d) -> p h d", h=nh),
                                      AX, ALU.add).then_inc(g_ss, 1)
                dve.wait_ge(g_rt, NI[g] + 1)
                if NB0[g] > 0:
                    dve.wait_ge(g_kn, NB0[g])
                own.link(dve.reciprocal(gs[:, 2, 0:T, 0:nh], gs[:, 1, 0:T, 0:nh]))
                if NLAST[g] is not None and NLAST[g] != GI["qm0"]:
                    dve.wait_ge(g_tp, NB0[g])
                for t in range(T):
                    dve.tensor_tensor(kn[:, t, :].rearrange("p (h d) -> p h d", h=nh),
                                      gset(g)[t][:].rearrange("p (h d) -> p h d", h=nh),
                                      gs[:, 2, t, 0:nh].unsqueeze(2).broadcast_to([P, nh, hd]),
                                      ALU.mult).then_inc(g_kn, 1)

            def values_copy(g):
                name, _, T, _ = GROUPS[g]
                dve.wait_ge(w_used, chunk_of(name, 3) + 1)
                for t in range(T):
                    dst = {"memV0": Vm0[:, t % MT, :], "memV1": Vm1[:, t % MT, :],
                           "v": V[:, t, 0:512], "v'": V[:, t, 512:1024]}[name]
                    dve.tensor_copy(dst, gset(g)[t][:]).then_inc(v_ev, 1)

            def conv_xr(i):
                dve.wait_ge(xc_0, i + 1)
                for n, tap in enumerate((2, 1, 0)):
                    sh = 3 - tap
                    ins = dve.scalar_tensor_tensor(out=xc[:, i, sh:SEQ], in0=bank[4 + i % 2][:, 0:SEQ - sh],
                                                   scalar=col("conv_a", 5 * i + tap), in1=xc[:, i, sh:SEQ],
                                                   op0=ALU.mult, op1=ALU.add)
                    if tap:
                        own.link(ins)
                    else:
                        ins.then_inc(xc_done, 1)

            def conv_low(i):
                dve.wait_ge(xc_hi, i + 1)
                dve.wait_ge(xc_done, i + 1)
                dve.tensor_tensor(mid_lo[:, i, :], xc[:, i, :], mid_hi[:, i, :].bitcast(F32), ALU.subtract)\
                    .then_inc(xc_lo, 1)

            def ma_max(L, h):
                u = MH * L + h
                for half in range(2):
                    dve.wait_ge(ma_s, 2 * u + half + 1)
                    if u > 0:
                        dve.wait_ge(ma_e, TT * u)
                    own.inc(dve.tensor_reduce(mx[:, 0, 0, 2 * half:2 * half + 2],
                                              bank[6 + half][:].rearrange("p (t m) -> p t m", t=2), AX, ALU.max))
                own.wait()
                dve.tensor_scalar(nmx[:, 0, :], mx[:, 0, 0, :], -MHD ** -0.5, None, ALU.mult).then_inc(ma_nm, 1)

            def ma_scale(L, h):
                u = MH * L + h
                Pm = Pm0 if L == 0 else Pm1
                dve.wait_ge(ma_e, TT * (u + 1))
                if u > 0:
                    dve.wait_ge(ma_p, u)
                dve.reciprocal(mx[:, 0, 2, :], mx[:, 0, 1, :]).then_inc(ma_rs, 1)
                dve.wait_ge(ma_rs, u + 1)
                for t in range(TT):
                    ins = dve.tensor_scalar(Pm[:, t, :], Pm[:, t, :], mx[:, 0, 2, t:t + 1], None, ALU.mult)
                ins.then_inc(ma_p, 1)

            def ma_copy(L, h):
                u = MH * L + h
                PTm = PTm0 if L == 0 else PTm1
                dve.wait_ge(ma_t, u + 1)
                if u > 0:
                    dve.wait_ge(ma_pv, u)
                for m in range(MT):
                    ins = dve.tensor_copy(PTm[:, m, :], bank[m][:])
                ins.then_inc(ma_pt, 1)

            def ma_low(L, h):
                u = MH * L + h
                k = (RT, KT)[L] + h
                dve.wait_ge(ma_hi, u + 1)
                dve.tensor_tensor(mid_lo[:, k, :], bank[2 + h % 2][:], mid_hi[:, k, :].bitcast(F32),
                                  ALU.subtract).then_inc(ma_lo, 1)

            def ca_add_bias(a):
                dve.wait_ge(strip_in[a % 2], 16 * (a // 2 + 1))
                if a >= 2:
                    dve.wait_ge(ca_t, a - 1)
                    dve.wait_ge(ca_e, TT * (a - 1))
                at = 0
                for t in range(TT):
                    n = P * (t + 1)
                    dve.wait_ge(ca_s, TT * a + t + 1)
                    dve.tensor_tensor_reduce(Sc[:, a % 2, at:at + n], bank[4 + t][:, 0:n],
                                             strip[:, a % 2, SEQ - n:SEQ], 1.0, -3.0e38, ALU.add, ALU.max,
                                             mx[:, a % 2, 0, t:t + 1]).then_inc(ca_add, 1)
                    at += n
                dve.wait_ge(ca_add, TT * (a + 1))
                dve.tensor_scalar(nmx[:, a % 2, :], mx[:, a % 2, 0, :], -1.0, None, ALU.mult).then_inc(ca_nm, 1)

            def ca_scale(a):
                dve.wait_ge(ca_e, TT * (a + 1))
                dve.reciprocal(mx[:, a % 2, 2, :], mx[:, a % 2, 1, :]).then_inc(ca_rs, 1)
                dve.wait_ge(ca_rs, a + 1)
                at = 0
                for t in range(TT):
                    n = P * (t + 1)
                    ins = dve.tensor_scalar(Sc[:, a % 2, at:at + n], Sc[:, a % 2, at:at + n],
                                            mx[:, a % 2, 2, t:t + 1], None, ALU.mult)
                    at += n
                ins.then_inc(ca_p, 1)

            def ca_copy(a):
                dve.wait_ge(ca_t, a + 1)
                if a > 0:
                    dve.wait_ge(ca_pv, a)
                dve.tensor_copy(PTs[:, 512:1024], bank[1][:]).then_inc(ca_ptd, 1)
                dve.tensor_copy(PTs[:, 1024:1280], bank[2][:, 0:256]).then_inc(ca_ptd, 1)

            def ca_low(p):
                dve.wait_ge(ca_hi, p + 1)
                dve.tensor_tensor(mid_lo[:, p, :], bank[3][:], mid_hi[:, p, :].bitcast(F32), ALU.subtract)\
                    .then_inc(ca_lo, 1)

            def out_steps(name, stat_base):
                with dve.Fori(0, KT // 2) as i:
                    for m in range(2):
                        dve.wait_ge(w_used, RING * i + (BASE[name] + 2 * m + 2))
                        dve.tensor_tensor(xT[:, bass.ds(2 * i + m, 1), :], xT[:, bass.ds(2 * i + m, 1), :],
                                          bank[4 + m][:].unsqueeze(1), ALU.add).then_inc(o_add, 1)
                        if stat_base is not None:
                            add_square(stat_base, m, SEQ, i, 2)

            def up_steps(name):
                U = UI[name]
                L = name[2]
                q0 = FH * (U % 2)
                with dve.Fori(0, FH // 2) as i:
                    own.enter(i, 4)
                    for p in range(2):
                        n = FH * U + p
                        for s, acc in ((0, uc), (1, gc)):
                            dve.wait_ge(up_first, RING * i + (2 * n + s + 1))
                            f = COLS["ffn" + L] + 8 * (q0 + p) + 4 * s
                            own.link(dve.scalar_tensor_tensor(
                                out=acc[:, p, 1:SEQ], in0=bank[2 * s + p][:, 0:SEQ - 1],
                                scalar=cols[:, bass.ds(16 * i + (f + 1), 1)], in1=acc[:, p, 1:SEQ],
                                op0=ALU.mult, op1=ALU.add))
                            dve.scalar_tensor_tensor(
                                out=acc[:, p, 2:SEQ], in0=bank[2 * s + p][:, 0:SEQ - 2],
                                scalar=cols[:, bass.ds(16 * i + (f + 2), 1)], in1=acc[:, p, 2:SEQ],
                                op0=ALU.mult, op1=ALU.add).then_inc(up_conv, 1)
                        dve.wait_ge(up_gelu, 2 * i + (n + 1))
                        dve.wait_ge(up_conv, RING * i + (2 * n + 2))
                        dve.tensor_tensor(uc[:, p, :], uc[:, p, :], gc[:, p, :], ALU.mult).then_inc(up_hid, 1)
                        dve.wait_ge(up_hi, 2 * i + (n + 1))
                        dve.tensor_tensor(mid_lo[:, bass.ds(2 * i + p, 1), :], uc[:, p, :].unsqueeze(1),
                                          mid_hi[:, bass.ds(2 * i + p, 1), :].bitcast(F32), ALU.subtract)\
                            .then_inc(up_lo, 1)
                    own.leave(FH // 2)

            def log_sigmoid():
                e, t, y, z, p, r = (lsc[:, n, :] for n in (1, 2, 3, 4, 5, 6))
                dve.wait_ge(lam_e, 2)
                own.link(dve.tensor_scalar(t, e, 2.0, None, ALU.add))
                own.link(dve.reciprocal(r, t))
                own.link(dve.tensor_tensor(y, e, r, ALU.mult))
                own.link(dve.tensor_tensor(z, y, y, ALU.mult))
                own.link(dve.tensor_scalar(p, z, 1.0 / 17, 1.0 / 15, ALU.mult, ALU.add))
                for n in range(13, 0, -2):
                    own.link(dve.tensor_tensor(p, p, z, ALU.mult))
                    own.link(dve.tensor_scalar(p, p, 1.0 / n, None, ALU.add))
                own.link(dve.tensor_tensor(p, p, y, ALU.mult))
                own.link(dve.tensor_scalar(p, p, 2.0 * RG_C, None, ALU.mult))
                own.link(dve.tensor_scalar(t, col_n("lam", RT), 0.0, RG_C, ALU.min, ALU.mult))
                dve.tensor_tensor(lsc[:, 7, :], t, p, ALU.subtract).then_inc(lam_c, 1)

            dve.memset(eps[:], EPS)
            dve.memset(ones[:], 1.0).then_inc(ones_ok, 1)
            clear_sum("mem")
            for k in range(KT):
                add_square(0, k, MEM)
            dve.wait_ge(const_in, 32)
            stat("mem", MEM)
            clear_sum("mix0")
            for k in range(KT):
                add_square(KT, k, SEQ)
            norm("mem0", "g_mem0", "mem")
            stat("mix0", SEQ)
            norm("mix0", "g_mix0", "mix0")
            dve.tensor_scalar(gqs[:], col("g_qa"), AHD ** -0.5, None, ALU.mult).then_inc(gq_ok, 1)
            log_sigmoid()
            group_norm(GI["memK0"])
            values_copy(GI["memV0"])
            group_norm(GI["qm0"])
            for i in range(RT):
                conv_xr(i)
                if i >= 1:
                    conv_low(i - 1)
                if 4 <= i < 4 + MH:
                    ma_low(0, i - 4)
                if 3 <= i < 3 + MH:
                    ma_copy(0, i - 3)
                if 2 <= i < 2 + MH:
                    ma_max(0, i - 2)
                    ma_scale(0, i - 2)
            conv_low(RT - 1)
            for half in range(2):
                for t in range(5):
                    m = 5 * half + t
                    dve.wait_ge(gt_sig, m + 1)
                    dve.tensor_tensor(I[:, t, :], I[:, t, :], xc[:, m, :], ALU.mult).then_inc(gt_ix, 1)
                for t in range(5):
                    m = 5 * half + t
                    dve.wait_ge(gt_exp, 2 * m + 2)
                    if m >= 2:
                        dve.wait_ge(gt_v, m - 1)
                    own.link(dve.tensor_tensor(tmp[:, t % 2], Aa[:, t, :], Aa[:, t, :], ALU.mult))
                    dve.scalar_tensor_tensor(out=R[:, t, :], in0=tmp[:, t % 2], scalar=1.0, in1=R[:, t, :],
                                             op0=ALU.add, op1=ALU.mult).then_inc(gt_v, 1)
                if half:
                    for m in range(5):
                        gate_low(dve, m)
                for t in range(5):
                    m = 5 * half + t
                    dve.wait_ge(gt_root, m + 1)
                    dve.wait_ge(gt_ix, m + 1)
                    own.link(dve.tensor_tensor(I[:, t, :], I[:, t, :], R[:, t, :], ALU.mult))
                    own.link(dve.tensor_tensor_scan(R[:, t, :], Aa[:, t, :], I[:, t, :], 0.0, ALU.mult, ALU.add))
                    dve.wait_ge(yg_gelu, m + 1)
                    dve.tensor_tensor(xc[:, m, :], R[:, t, :], gy[:, m, :], ALU.mult).then_inc(gt_main, 1)
                    if half and t >= 1:
                        gate_low(dve, m - 1)
            gate_low(dve, RT - 1)
            clear_sum("ffn0")
            out_steps("out0", SQ["out0"])
            stat("ffn0", SEQ)
            norm("ffn0", "g_ffn0", "ffn0")
            up_steps("up00")
            out_steps("down00", None)
            up_steps("up01")
            clear_sum("kv")
            out_steps("down01", SQ["down01"])
            norm("mem1", "g_mem1", "mem")
            stat("kv", SEQ)
            norm("kv", "g_kv", "kv")
            norm("mix1", "g_mix1", "kv")
            group_norm(GI["memK1"])
            values_copy(GI["memV1"])
            group_norm(GI["k"])
            group_norm(GI["k'"])
            values_copy(GI["v"])
            values_copy(GI["v'"])
            group_norm(GI["q"])
            group_norm(GI["q'"])
            group_norm(GI["qm1"])
            for i in range(MH + 2):
                if i >= 2:
                    ma_low(1, i - 2)
                if 1 <= i <= MH:
                    ma_copy(1, i - 1)
                if i < MH:
                    ma_max(1, i)
                    ma_scale(1, i)
            for a in range(AH + 2):
                if a >= 4 and a % 2 == 0:
                    ca_low(a // 2 - 2)
                if a >= 2:
                    ca_copy(a - 2)
                if a < AH:
                    ca_add_bias(a)
                if 1 <= a <= AH:
                    ca_scale(a - 1)
            ca_low(AH // 2 - 1)
            clear_sum("ffn1")
            out_steps("out1", SQ["out1"])
            stat("ffn1", SEQ)
            norm("ffn1", "g_ffn1", "ffn1")
            up_steps("up10")
            out_steps("down10", None)
            up_steps("up11")
            out_steps("down11", None)


def _feature_rows(a, n):
    import numpy as np
    return np.ascontiguousarray(a.reshape(a.shape[0], n, P).transpose(2, 1, 0))


def _stationary(w, order=None, chunks=1):
    import numpy as np
    K, M = w.shape
    w = w.reshape(K // P, P, M // P, P)
    if order is not None:
        w = w[order]
    w = w.transpose(2, 1, 0, 3)
    w = w.reshape(M // P, P, chunks, K // chunks).transpose(0, 2, 1, 3)
    return np.ascontiguousarray(w.reshape(M // P * chunks, P, K // chunks))


def _moving(w):
    import numpy as np
    G = w.shape[1] // 512
    w = w.reshape(4, 2, P, G, 512).transpose(3, 0, 2, 1, 4)
    return np.ascontiguousarray(w.reshape(G * 4, P, 1024))


def _gates(w_r, w_i):
    import numpy as np
    dense = np.zeros((2, D_RNN, D_RNN), np.float32)
    for g, w in enumerate((w_r, w_i)):
        for b in range(D_RNN // RGB):
            dense[g, b * RGB:(b + 1) * RGB, b * RGB:(b + 1) * RGB] = w[b]
    out = np.zeros((RT, P, WIDTH["gates"] * P), np.float32)
    for m in range(RT):
        ks = gate_k(m)
        for g in range(2):
            for n, k in enumerate(ks):
                q = g * len(ks) + n
                out[m, :, q * P:(q + 1) * P] = dense[g, k * P:(k + 1) * P, m * P:(m + 1) * P]
    return out


def _strips(rel_bias):
    import numpy as np
    p, w = np.arange(P)[:, None], np.arange(SEQ)[None, :]
    rel = np.clip(p - (w - (SEQ - P)), -63, 256) + 63
    s = rel_bias[:, rel]
    s[:, 0:64, SEQ - 64:SEQ] = MASKED
    return np.ascontiguousarray(s)


def _columns(d):
    import numpy as np
    col = lambda v: v.reshape(-1, P).T
    parts = {"conv_a": np.stack([*(col(d["w_conv_a"][0, t]) for t in range(4)), col(d["b_conv_a"][0])], 2)
             .reshape(P, 5 * RT), "b_r": col(d["b_r_a"][0]), "b_i": col(d["b_i_a"][0]), "lam": col(d["lam_a"][0]),
             "g_kv": col(d["g_kv"]), "g_qa": np.tile(d["g_q_att"][0], 2)[:, None],
             "g_ka": np.tile(d["g_k_att"], 2)[:, None]}
    for L in range(2):
        parts["g_mix%d" % L] = col(d["g_mix"][L])
        parts["g_mem%d" % L] = col(d["g_mem"][L])
        parts["g_ffn%d" % L] = col(d["g_ffn"][L])
        parts["g_qm%d" % L] = d["g_q_mem"][L][:, None]
        parts["g_km%d" % L] = d["g_k_mem"][L][:, None]
        w, b = d["w_dw_ffn"][L], d["b_dw_ffn"][L]
        taps = [col(w[2]), col(w[1]), col(w[0]), col(b)]
        both = [t[:, s * FT:(s + 1) * FT] for s in range(2) for t in taps]
        parts["ffn%d" % L] = np.stack(both, 2).reshape(P, 8 * FT)
    out = np.zeros((P, NCOLS), np.float32)
    for name, at in COLS.items():
        out[:, at:at + parts[name].shape[1]] = parts[name]
    return out


def kernel(**inputs):
    import numpy as np
    import concourse.bacc as bacc
    from concourse.bass_utils import run_bass_kernel_spmd

    d = {k: np.asarray(v) for k, v in inputs.items()}
    arrays = {"xT": _feature_rows(d["x"][0], KT), "memT": _feature_rows(d["mem"][0], KT),
              "cols": _columns(d), "ident": np.eye(P, dtype=np.float32), "strips": _strips(d["rel_bias_b"][0])}
    w = d["w_in_a"][0]
    arrays["w_xr"] = _stationary(w[:, 0:D_RNN])
    arrays["w_yg"] = _stationary(w[:, D_RNN:2 * D_RNN])
    arrays["w_qm0"] = _moving(w[:, 2 * D_RNN:])
    arrays["w_gates"] = _gates(d["w_r_a"][0], d["w_i_a"][0])
    arrays["w_out0"] = _stationary(d["w_out_a"][0], OUT0_ORDER, 2)
    arrays["w_out1"] = _stationary(d["w_out_b"][0], None, 2)
    arrays["w_k"] = _moving(d["w_kv"][:, 0:D])
    arrays["w_v"] = _moving(d["w_kv"][:, D:])
    arrays["w_q"] = _moving(d["w_in_b"][0][:, 0:D])
    arrays["w_qm1"] = _moving(d["w_in_b"][0][:, D:])
    for L in range(2):
        arrays["w_memK%d" % L] = _moving(d["w_mem_kv"][L][:, 0:512])
        arrays["w_memV%d" % L] = _moving(d["w_mem_kv"][L][:, 512:])
        up = _stationary(d["w_up"][L])
        for f in range(2):
            pairs = [t for p in range(FH) for t in (FH * f + p, FT + FH * f + p)]
            arrays["w_up%d%d" % (L, f)] = np.ascontiguousarray(up[pairs])
            rows = d["w_down"][L][FH * f * P:FH * (f + 1) * P]
            arrays["w_down%d%d" % (L, f)] = _stationary(rows, None, 2)
    nc = bacc.Bacc("TRN2", target_bir_lowering=False, num_devices=1, dynamic_dma_scratch_size=1024)
    A = {n: nc.dram_tensor("in_" + n, a.shape, F32, kind="ExternalInput").ap() for n, a in arrays.items()}
    out = nc.dram_tensor("out", (P, KT, SEQ), F32, kind="ExternalOutput").ap()
    build(nc, A, out)
    r = run_bass_kernel_spmd(nc, [{"in_" + n: a for n, a in arrays.items()}], core_ids=[0])
    y = np.asarray(r.results[0]["out"])
    return np.ascontiguousarray(y.transpose(2, 1, 0).reshape(1, SEQ, D))
```

```python
from contextlib import ExitStack

import concourse.bass as bass
from concourse import mybir

P = 128
F32 = mybir.dt.float32
F32R = mybir.dt.float32r
ALU = mybir.AluOpType
ACT = mybir.ActivationFunctionType
AX = mybir.AxisListType.X

SEQ, D = 512, 1024
KT = D // P
TT = SEQ // P
MEM, MT = 256, 2
MH, MHD = 4, 128
AH, AHD = 16, 64
D_RNN, RT = 1280, 10
RGB = 80
D_FF, FT = 3072, 24
FH = FT // 2
MID = 14
EPS = 1e-6
RG_C = 8.0
OUT0_ORDER = list(range(10, 14)) + list(range(10))
MASKED = -1e30

PHASES = [
    ("memK0", 4, 8), ("memV0", 4, 8), ("qm0", 4, 8), ("xr", RT, 8), ("gy", 2 * RT, 8), ("out0", 16, 7),
    ("up00", 24, 8), ("down00", 16, 6), ("up01", 24, 8), ("down01", 16, 6),
    ("memK1", 4, 8), ("memV1", 4, 8), ("k", 8, 8), ("v", 8, 8), ("q", 8, 8), ("qm1", 4, 8),
    ("out1", 16, 6),
    ("up10", 24, 8), ("down10", 16, 6), ("up11", 24, 8), ("down11", 16, 6),
]
BASE = {}
_at = 0
for _name, _n, _w in PHASES:
    BASE[_name] = _at
    _at += _n
CHUNKS = _at
WIDTH = {name: w for name, _, w in PHASES}
COUNT = {name: n for name, n, _ in PHASES}
RAW = 2
RING = 4
AHEAD = RING - 1

BATCH = RT // 2
GY = ([("g", i) for i in range(BATCH)] + [("y", 0), ("y", 1)]
      + [("g", i) for i in range(BATCH, RT - 2)] + [("y", 2)] + [("g", RT - 2), ("g", RT - 1)]
      + [("y", i) for i in range(3, RT)])

COLS = {}
_at = 0
for _name, _n in [("g_mix0", KT), ("g_mix1", KT), ("g_mem0", KT), ("g_mem1", KT), ("g_kv", KT),
                  ("g_ffn0", KT), ("g_ffn1", KT), ("conv_a", 5 * RT), ("b_r", RT), ("b_i", RT),
                  ("lam", RT), ("g_qm0", 1), ("g_km0", 1), ("g_qm1", 1), ("g_km1", 1),
                  ("g_qa", 1), ("g_ka", 1), ("ffn0", 8 * FT), ("ffn1", 8 * FT)]:
    COLS[_name] = _at
    _at += _n
NCOLS = _at


def gate_k(m):
    first = (P * m) // RGB * RGB
    last = -(-(P * m + P) // RGB) * RGB
    return list(range(first // P, -(-last // P)))


def steps(eng, n, body, peel_first=False, last=None):
    if peel_first:
        body(0)
    with eng.Fori(1 if peel_first else 0, n - (last is not None)) as i:
        body(i)
    if last is not None:
        last(n - 1)


class Tally:

    def __init__(self, eng, sem):
        self.eng, self.sem, self.n = eng, sem, 0

    def inc(self, ins):
        ins.then_inc(self.sem, 1)
        self.n += 1

    def wait(self):
        self.eng.wait_ge(self.sem, self.n)

    def link(self, ins):
        self.inc(ins)
        self.wait()


def build(nc, A, out):
    with ExitStack() as ctx:
        def sb(name, shape, dt=F32, stack=ctx, **kw):
            return stack.enter_context(nc.sbuf_tensor(name, shape, dt, **kw))

        def sem(name):
            return ctx.enter_context(nc.semaphore(name))

        xT = sb("xT", [P, KT, SEQ])
        mid_hi = sb("mid_hi", [P, MID, SEQ], F32R)
        mid_lo = sb("mid_lo", [P, MID, SEQ], F32R)
        raw = sb("raw", [P, RAW, 8 * P])
        whi = sb("whi", [P, RING, 8 * P], F32R)
        wlo = sb("wlo", [P, RING, 8 * P], F32R)
        cols = sb("cols", [P, NCOLS])
        ident = sb("ident", [P, P])
        ones = sb("ones", [P, P])
        work = sb("work", [P, 6, SEQ])
        sq, tmp, ssum = work[:, 0:2, :], work[:, 2:4, :], work[:, 4, :]
        diag = work[:, 5, :].rearrange("p (t c) -> p t c", c=P)
        Aa, a2 = work[:, 0:5, :], work[:, 5, :]
        rb = sb("rb", [P, SEQ])
        root = sb("root", [P, TT])
        rcol = sb("rcol", [P, TT])
        rcol_mem = sb("rcol_mem", [P, TT])
        gs = sb("gs", [P, 3, TT, 8])
        mx = sb("mx", [P, 3, 3, TT])
        nmx = sb("nmx", [P, 3, TT])
        lsc = sb("lsc", [P, 8, RT])
        eps = sb("eps", [P, 1])
        gqs = sb("gqs", [P, 1])
        right = ExitStack()
        hh = sb("hh", [P, KT, SEQ], F32R, right, side="right")
        hl = sb("hl", [P, KT, SEQ], F32R, right, side="right")
        right.close()
        right = ExitStack()
        qT = sb("qT", [P, KT, SEQ], F32, right, side="right")
        qmT1 = sb("qmT1", [P, MH, SEQ], F32, right, side="right")
        PTs = sb("PTs", [P, 1280], F32, right, side="right")
        right.close()
        right = ExitStack()
        sb("keep_right", [P, 2 * KT, SEQ], F32, right, side="right")
        ph = ExitStack()
        mh_hi = sb("mh_hi", [P, KT, MEM], F32R, ph)
        mh_lo = sb("mh_lo", [P, KT, MEM], F32R, ph)
        zf = sb("zf", [P, 4, SEQ], F32, ph)
        cf = sb("cf", [P, 4, SEQ], F32, ph)
        ph.close()
        ph = ExitStack()
        xc = sb("xc", [P, RT, SEQ], F32, ph)
        ph2 = ExitStack()
        gy = sb("gy", [P, RT, SEQ], F32, ph2)
        R = sb("R", [P, BATCH, SEQ], F32, ph2)
        I = sb("I", [P, BATCH, SEQ], F32, ph2)
        ph2.close()
        kn0 = sb("kn0", [P, TT, SEQ], F32, ph)
        qmT0 = sb("qmT0", [P, MH, SEQ], F32, ph)
        kmT0 = sb("kmT0", [P, MH, MEM], F32, ph)
        Vm0 = sb("Vm0", [P, MT, SEQ], F32, ph)
        memT = sb("memT", [P, KT, MEM], F32, ph)
        PTm0 = kn0[:, 0:MT, :]
        Pm0 = kn0[:, MT:TT, :].rearrange("p a b -> p (a b)").rearrange("p (t m) -> p t m", m=MEM)
        ph.close()
        ph = ExitStack()
        V = sb("V", [P, TT, D], F32, ph)
        kT = sb("kT", [P, KT, SEQ], F32, ph)
        kmT1 = sb("kmT1", [P, MH, MEM], F32, ph)
        Vm1 = sb("Vm1", [P, MT, SEQ], F32, ph)
        ph2 = ExitStack()
        kn1 = sb("kn1", [P, TT, SEQ], F32, ph2)
        ph2.close()
        Sc = sb("Sc", [P, 3, 1280], F32, ph)
        knq = sb("knq", [P, 2, SEQ], F32, ph)
        ph.close()
        right.close()
        strip = tmp

        bank = [ctx.enter_context(nc.psum_tensor(f"bank{i}", [P, 512], F32)) for i in range(8)]

        raw_in = [sem(f"raw_in{i}") for i in range(RAW)]
        w_hi, w_lo, w_used = sem("w_hi"), sem("w_lo"), sem("w_used")
        x_in, mem_in = [sem("x_in0"), sem("x_in1")], [sem("mem_in0"), sem("mem_in1")]
        mem_again, cols_in, ident_in, y_out = (sem(x) for x in ("mem_again", "cols_in", "ident_in", "y_out"))
        strip_in = [sem("strip_in0"), sem("strip_in1")]
        ones_ok, gq_ok, ma_rs = sem("ones_ok"), sem("gq_ok"), sem("ma_rs")
        sq_ready, sq_added = sem("sq_ready"), sem("sq_added")
        st_cols, st_root, st_diag, st_bcast, st_rb = (sem(x) for x in (
            "st_cols", "st_root", "st_diag", "st_bcast", "st_rb"))
        h_hi, h_lo = sem("h_hi"), sem("h_lo")
        g_sq, g_ss, g_rt, g_kn, g_tp, g_ev, v_ev = (sem(x) for x in (
            "g_sq", "g_ss", "g_rt", "g_kn", "g_tp", "g_ev", "v_ev"))
        xr_z, yg_z, gt_h = sem("xr_z"), sem("yg_z"), sem("gt_h")
        xc_0, xc_done, xc_hi, xc_lo = (sem(x) for x in ("xc_0", "xc_done", "xc_hi", "xc_lo"))
        yg_gelu = sem("yg_gelu")
        gt_sig, gt_ix, gt_exp, gt_v, gt_root, gt_lo = (sem(x) for x in (
            "gt_sig", "gt_ix", "gt_exp", "gt_v", "gt_root", "gt_lo"))
        lam_e = sem("lam_e")
        lam_c = sem("lam_c")
        ma_s, ma_nm, ma_e, ma_p, ma_t, ma_pt, ma_pv, ma_hi, ma_lo = (sem("ma_" + x) for x in (
            "s", "nm", "e", "p", "t", "pt", "pv", "hi", "lo"))
        at_s, at_add, at_nm, at_e, at_rs, at_p, at_t, at_pta, at_ptd, at_pv, at_hi, at_lo = (
            sem("at_" + x) for x in (
                "s", "add", "nm", "e", "rs", "p", "t", "pta", "ptd", "pv", "hi", "lo"))
        up_z, up_first, up_conv, up_gelu, up_hid, up_hi, up_lo = (sem("up_" + x) for x in (
            "z", "first", "conv", "gelu", "hid", "hi", "lo"))
        o_add = sem("o_add")
        st_rc, up_tap = sem("st_rc"), sem("up_tap")
        dve_own = sem("dve_own")

        H = {n: i for i, n in enumerate(["mem0", "mix0", "ffn0", "mem1", "kv", "mix1", "ffn1"])}
        ST = {n: i for i, n in enumerate(["mem", "mix0", "ffn0", "kv", "ffn1"])}
        BC = {n: i for i, n in enumerate(["mix0", "ffn0", "ffn1"])}
        GROUPS = [("memK0", "mem0", MT, MHD), ("memV0", "mem0", MT, 0), ("qm0", "mix0", TT, MHD),
                  ("memK1", "mem1", MT, MHD), ("memV1", "mem1", MT, 0),
                  ("k", "kv", TT, AHD), ("k'", "kv", TT, AHD), ("v", "kv", TT, 0), ("v'", "kv", TT, 0),
                  ("q", "mix1", TT, AHD), ("q'", "mix1", TT, AHD), ("qm1", "mix1", TT, MHD)]
        GI = {g[0]: i for i, g in enumerate(GROUPS)}
        GT0, NB0, VB0, NI = [], [], [], []
        a = b = c = d = 0
        for _, _, t, hd in GROUPS:
            GT0.append(a); NB0.append(b); VB0.append(c); NI.append(d)
            a += t
            if hd:
                b += t
                d += 1
            else:
                c += t
        NLAST = {}
        prev = None
        for i, g in enumerate(GROUPS):
            NLAST[i] = prev
            if g[3]:
                prev = i

        SETS = {"memK0": 0, "memV0": 2, "qm0": 4, "memK1": 0, "memV1": 2, "k": 4, "k'": 0, "v": 4,
                "v'": 0, "q": 4, "q'": 0, "qm1": 4}
        BEFORE = {"k'": ["memK1", "memV1"], "v": ["k"], "v'": ["k'"], "q": ["v"], "q'": ["v'"], "qm1": ["q"]}

        SUM_BANK = {n: bank[2 if n == "mix0" else 6] for n in ST}
        BCAST_BANK = {n: bank[3 if n == "mix0" else 7] for n in BC}

        Y_BANK = [0, 1] + [i % 4 for i in range(4, RT + 2)]
        Y_FREE = [(xr_z, RT - 1), (xr_z, RT), (yg_z, 1), (yg_z, 2), (gt_sig, RT), (gt_sig, RT)] \
            + [(yg_z, i - 3) for i in range(6, RT)]

        def gset(i):
            b = SETS[GROUPS[i][0]]
            return bank[b:b + GROUPS[i][2]]

        def rows(g, t):
            if g == GI["qm1"]:
                return work[:, 4 + t, :] if t < 2 else knq[:, t - 2, :]
            return (kn0 if g < GI["memK1"] else kn1)[:, t, :]

        def chunk_of(name, j=0):
            second = name.endswith("'")
            return BASE[name.rstrip("'")] + 4 * second + j

        HDST = {"mem0": (mh_hi, mh_lo), "mem1": (mh_hi, mh_lo),
                "mix0": (hh, hl), "ffn0": (hh, hl), "kv": (hh, hl), "ffn1": (hh, hl),
                "mix1": (mid_hi, mid_lo)}
        GAIN = {"mem0": "g_mem0", "mem1": "g_mem1", "mix0": "g_mix0", "ffn0": "g_ffn0", "kv": "g_kv",
                "ffn1": "g_ffn1", "mix1": "g_mix1"}
        HEADS = [("c", a) for a in range(AH)] + [("m", h) for h in range(MH)]
        OUTPUTS = [s for s, (kind, h) in enumerate(HEADS) if kind == "m" or h % 2]
        OTILE = [KT + h if kind == "m" else h // 2 for kind, h in (HEADS[s] for s in OUTPUTS)]

        def col(name, j=0):
            return cols[:, COLS[name] + j:COLS[name] + j + 1]

        def col_n(name, n):
            return cols[:, COLS[name]:COLS[name] + n]

        def conv_high(act, i):
            act.wait_ge(xc_done, i + 1)
            act.activation(mid_hi[:, i, :], xc[:, i, :], ACT.Copy).then_inc(xc_hi, 1)

        OUTS = ["out0", "down00", "down01", "out1", "down10", "down11"]
        OI = {n: KT * i for i, n in enumerate(OUTS)}
        OUT_BANK = {n: 0 if n == "out1" else 4 for n in OUTS}
        UPS = ["up00", "up01", "up10", "up11"]
        UI = {n: i for i, n in enumerate(UPS)}
        SQ = {"mem": 0, "mix0": KT, "out0": 2 * KT, "down01": 3 * KT, "out1": 4 * KT}

        block = ctx.enter_context(nc.Block())

        @block.sync
        def _(sp):
            sp.dma_start(cols[:], A["cols"]).then_inc(cols_in, 16)
            sp.dma_start(raw[:, 0], A["w_memK0"][0]).then_inc(raw_in[0], 16)
            sp.dma_start(memT[:, 0:4], A["memT"][:, 0:4]).then_inc(mem_in[0], 16)
            sp.dma_start(raw[:, 1], A["w_memK0"][1]).then_inc(raw_in[1], 16)
            sp.dma_start(memT[:, 4:8], A["memT"][:, 4:8]).then_inc(mem_in[1], 16)
            for n in range(2):
                sp.dma_start(xT[:, 4 * n:4 * n + 4], A["xT"][:, 4 * n:4 * n + 4]).then_inc(x_in[n], 16)
                c = RAW + n
                sp.wait_ge(w_lo, c - RAW + 1)
                sp.dma_start(raw[:, c % RAW], A["w_memK0"][c]).then_inc(raw_in[c % RAW], 16)
            sp.dma_start(ident[:], A["ident"]).then_inc(ident_in, 16)

            def load(name, first, n):
                with sp.Fori(first // RAW, n // RAW) as i:
                    for j in range(RAW):
                        c = BASE[name] + j
                        sp.wait_ge(w_lo, RAW * i + (c - RAW + 1))
                        sp.dma_start(raw[:, c % RAW, 0:WIDTH[name] * P], A["w_" + name][RAW * i + j])\
                            .then_inc(raw_in[c % RAW], 16)

            for name, n, _ in PHASES[1:]:
                if name == "up01":
                    sp.wait_ge(w_used, BASE["up00"])
                    sp.dma_start(memT[:], A["memT"]).then_inc(mem_again, 16)
                if name != "out1":
                    load(name, 0, n)
                    continue
                load(name, 0, RING)
                sp.wait_ge(up_lo, 2 * FH)
                for a in range(AH):
                    if a >= 2:
                        sp.wait_ge(at_add, TT * (a - 1))
                    sp.dma_start(strip[:, a % 2], A["strips"][a]).then_inc(strip_in[a % 2], 16)
                load(name, RING, n)
            for k in range(KT):
                sp.wait_ge(o_add, OI["down11"] + k + 1)
                sp.dma_start(out[:, k], xT[:, k]).then_inc(y_out, 16)
            sp.wait_ge(y_out, 16 * KT)

        @block.gpsimd
        def _(pool):
            def split_lo(i, j):
                pool.wait_ge(w_hi, RING * i + j + 1)
                nc.gpsimd.tensor_tensor(wlo[:, j], raw[:, j % RAW], whi[:, j].bitcast(F32), ALU.subtract)\
                    .then_inc(w_lo, 1)

            def split_chunks(first, last):
                whole = -(-first // RING)
                for c in range(first, RING * whole):
                    split_lo(c // RING, c % RING)
                with pool.Fori(whole, last // RING) as i:
                    for j in range(RING):
                        split_lo(i, j)
                for c in range(last - last % RING, last):
                    split_lo(c // RING, c % RING)

            def at_scale(s):
                kind, h = HEADS[s]
                pool.wait_ge(at_rs, s + 1)
                at = 0
                for t in range(TT):
                    n = MEM if kind == "m" else P * (t + 1)
                    ins = pool.tensor_tensor(Sc[:, s % 3, at:at + n], Sc[:, s % 3, at:at + n],
                                             mx[:, s % 3, 2, t:t + 1].broadcast_to([P, n]), ALU.mult)
                    at += n
                ins.then_inc(at_p, 1)

            pool.wait_ge(w_lo, 1)
            split_chunks(1, BASE["out1"] + AHEAD)
            for s in range(len(HEADS)):
                at_scale(s)
            split_chunks(BASE["out1"] + AHEAD, CHUNKS)

        @block.tensor
        def _(pe):
            def pass3(o, w_h, w_l, x_h, x_l, start, stop):
                nc.tensor.matmul(o, w_h, x_h, start=start, stop=False)
                nc.tensor.matmul(o, w_h, x_l, start=False, stop=False)
                return nc.tensor.matmul(o, w_l, x_h, start=False, stop=stop)

            def colsum(inst, n):
                pe.wait_ge(sq_added, KT * (ST[inst] + 1))
                if ST[inst] > 0:
                    pe.wait_ge(st_root, ST[inst])
                if inst == "mix0":
                    pe.wait_ge(v_ev, MT)
                for t in range(n // P):
                    mm = nc.tensor.matmul(SUM_BANK[inst][:, t:t + 1], ssum[:, t * P:(t + 1) * P], ones[:, 0:1],
                                          start=t == 0, stop=True, skip_group_check=True)
                mm.then_inc(st_cols, 1)

            def bcast(inst, n):
                pe.wait_ge(st_diag, BC[inst] + 1)
                nc.tensor.matmul(BCAST_BANK[inst][:, 0:n], ones[:], diag[:, 0:n // P, :], start=True, stop=True)\
                    .then_inc(st_bcast, 1)

            def free_set(g):
                for b in BEFORE.get(GROUPS[g][0], []):
                    b = GI[b]
                    if GROUPS[b][3]:
                        pe.wait_ge(g_ev, NB0[b] + GROUPS[b][2])
                    else:
                        pe.wait_ge(v_ev, VB0[b] + GROUPS[b][2])
                if g == GI["memK1"]:
                    pe.wait_ge(up_z, 2 * 2 * FH)
                if g == GI["qm0"]:
                    pe.wait_ge(st_root, 1)
                if g == GI["k"]:
                    pe.wait_ge(st_root, ST["kv"] + 1)
                    pe.wait_ge(o_add, OI["down01"] + KT)

            def group(g, hooks={}):
                name, inp, T, hd = GROUPS[g]
                dh, dl = HDST[inp]
                free_set(g)
                for j in range(4):
                    c = chunk_of(name, j)
                    pe.wait_ge(w_lo, c + 1)
                    for q in range(2):
                        k = 2 * j + q
                        pe.wait_ge(h_lo, KT * H[inp] + k + 1)
                        for t in range(T):
                            mm = pass3(gset(g)[t][:], dh[:, k, t * P:(t + 1) * P], dl[:, k, t * P:(t + 1) * P],
                                       whi[:, c % RING, q * 512:(q + 1) * 512],
                                       wlo[:, c % RING, q * 512:(q + 1) * 512], k == 0, k == KT - 1)
                    mm.then_inc(w_used, 1)
                    if j in hooks:
                        hooks[j]()

            def group_transposes(g):
                name, _, T, hd = GROUPS[g]
                for t in range(T):
                    pe.wait_ge(g_kn, NB0[g] + t + 1)
                    for f in range(4):
                        mm = nc.tensor.transpose(gset(g)[t][:, f * P:(f + 1) * P],
                                                 rows(g, t)[:, f * P:(f + 1) * P], ident[:])
                    mm.then_inc(g_tp, 1)

            def fm_tile(o, c, slot, inp, nk, free):
                dh, dl = HDST[inp]
                pe.wait_ge(w_lo, c + 1)
                if free is not None:
                    pe.wait_ge(*free)
                for k in range(nk):
                    mm = pass3(o, whi[:, slot, k * P:(k + 1) * P], wlo[:, slot, k * P:(k + 1) * P],
                               dh[:, k, :], dl[:, k, :], k == 0, k == nk - 1)
                mm.then_inc(w_used, 1)

            def ma_scores(u):
                if u == 0:
                    pe.wait_ge(g_ev, NB0[GI["qm0"]] + TT)
                for half in range(2):
                    if u > 0:
                        pe.wait_ge(ma_nm, u)
                        pe.wait_ge(ma_e, TT * (u - 1) + 2 * half + 2)
                    for t in range(2):
                        tt = 2 * half + t
                        mm = nc.tensor.matmul(bank[6 + half][:, t * MEM:(t + 1) * MEM],
                                              qmT0[:, u, tt * P:(tt + 1) * P], kmT0[:, u, :],
                                              start=t == 0, stop=True, skip_group_check=True)
                    mm.then_inc(ma_s, 1)

            def ma_transposes(u):
                pe.wait_ge(ma_p, u + 1)
                if u > 0:
                    pe.wait_ge(ma_pt, u)
                for m in range(MT):
                    for t in range(TT):
                        mm = nc.tensor.transpose(bank[4 + m][:, t * P:(t + 1) * P],
                                                 Pm0[:, t, m * P:(m + 1) * P], ident[:])
                mm.then_inc(ma_t, 1)

            def ma_values(u):
                pe.wait_ge(ma_pt, u + 1)
                if u > 1:
                    pe.wait_ge(ma_lo, u - 1)
                else:
                    pe.wait_ge(v_ev, VB0[GI["memV0"]] + MT)
                for m in range(MT):
                    mm = nc.tensor.matmul(bank[2 + u % 2][:], Vm0[:, m, u * MHD:(u + 1) * MHD],
                                          PTm0[:, m, :], start=m == 0, stop=m == MT - 1)
                mm.then_inc(ma_pv, 1)

            def at_scores(s):
                kind, h = HEADS[s]
                for t in range(TT):
                    if s >= 1:
                        pe.wait_ge(at_e if HEADS[s - 1][0] == "m" else at_add, TT * (s - 1) + t + 1)
                    if kind == "m":
                        mm = nc.tensor.matmul(bank[t][:, 0:MEM], qmT1[:, h, t * P:(t + 1) * P], kmT1[:, h, :],
                                              start=True, stop=True)
                    else:
                        n, p0 = P * (t + 1), AHD * (h % 2)
                        mm = nc.tensor.matmul(bank[t][:, 0:n], qT[p0:p0 + AHD, h // 2, t * P:(t + 1) * P],
                                              kT[p0:p0 + AHD, h // 2, 0:n], start=True, stop=True)
                    mm.then_inc(at_s, 1)

            PT_BANK = [(0, 0), (1, 0), (2, 0), (1, 384)]
            PT_AT = [0, 512, 1024, 896]

            def at_transposes(s):
                kind, h = HEADS[s]
                pe.wait_ge(at_p, s + 1)
                if s >= 1:
                    pe.wait_ge(at_pta, s)
                    pe.wait_ge(at_ptd, s)
                at = 0
                for t in range(TT):
                    for kt in range(MT if kind == "m" else t + 1):
                        b, o = (kt, t * P) if kind == "m" else (PT_BANK[kt][0], PT_BANK[kt][1] + (t - kt) * P)
                        mm = nc.tensor.transpose(bank[4 + b][:, o:o + P], Sc[:, s % 3, at:at + P], ident[:])
                        at += P
                mm.then_inc(at_t, 1)

            def at_values(s):
                kind, h = HEADS[s]
                pe.wait_ge(at_pta, s + 1)
                pe.wait_ge(at_ptd, s + 1)
                done = len([o for o in OUTPUTS if o < s])
                if done and (s - 1) in OUTPUTS:
                    pe.wait_ge(at_lo, done)
                if kind == "m":
                    for m in range(MT):
                        mm = nc.tensor.matmul(bank[7][:], Vm1[:, m, h * MHD:(h + 1) * MHD],
                                              PTs[:, m * SEQ:(m + 1) * SEQ], start=m == 0, stop=m == MT - 1)
                else:
                    p0 = AHD * (h % 2)
                    for kt in range(TT):
                        n = SEQ - kt * P
                        mm = nc.tensor.matmul(bank[7][p0:p0 + AHD, kt * P:SEQ], V[:, kt, h * AHD:(h + 1) * AHD],
                                              PTs[:, PT_AT[kt]:PT_AT[kt] + n], start=kt == 0, stop=kt == TT - 1)
                mm.then_inc(at_pv, 1)

            def out_proj(name, order, ready, hooks={}):
                nk = len(order)

                def body(i):
                    for m in range(2):
                        n = 0
                        for half in range(2):
                            c = BASE[name] + 2 * m + half
                            pe.wait_ge(w_lo, RING * i + c + 1)
                            if half == 0 and not (name in ("out0", "out1") and isinstance(i, int)):
                                pe.wait_ge(o_add, 2 * i + (OI[name] + m - 1))
                            for q in range(nk // 2):
                                if m == 0 and isinstance(i, int) and n in hooks:
                                    hooks[n]()
                                if m == 0 and n in ready:
                                    for w in ready[n]:
                                        pe.wait_ge(*w)
                                k = order[n]
                                mm = pass3(bank[OUT_BANK[name] + m][:], whi[:, c % RING, q * P:(q + 1) * P],
                                           wlo[:, c % RING, q * P:(q + 1) * P], mid_hi[:, k, :], mid_lo[:, k, :],
                                           n == 0, n == nk - 1)
                                n += 1
                            mm.then_inc(w_used, 1)
                steps(pe, KT // 2, body, name in ("out0", "out1"))

            def ffn_up(name):
                dh, dl = HDST["ffn" + name[2]]
                U = UI[name]
                inp = KT * H["ffn" + name[2]]
                def body(i):
                    for p in range(2):
                        for s in range(2):
                            c = BASE[name] + 2 * p + s
                            pe.wait_ge(w_lo, RING * i + c + 1)
                            if not (name == "up00" and isinstance(i, int)):
                                pe.wait_ge(up_z, RING * i + (2 * FH * U + 2 * p + s - 3))
                            if name == "up10" and isinstance(i, int) and s == 0:
                                pe.wait_ge(o_add, OI["out1"] + KT - 1 + p)
                            for k in range(KT):
                                if p == 0 and s == 0:
                                    pe.wait_ge(h_lo, inp + k + 1)
                                mm = pass3(bank[2 * s + p][:], whi[:, c % RING, k * P:(k + 1) * P],
                                           wlo[:, c % RING, k * P:(k + 1) * P], dh[:, k, :], dl[:, k, :],
                                           k == 0, k == KT - 1)
                            mm.then_inc(w_used, 1)
                            if name[3] == "0" and isinstance(i, int) and p == 0:
                                (colsum, bcast)[s]("ffn" + name[2], SEQ)
                steps(pe, FH // 2, body, name[3] == "0")

            def ffn_down(name):
                U = UI["up" + name[4:]]
                out_proj(name, list(range(FH)),
                         {0: [(up_lo, FH * U + FH - 1)], FH - 1: [(up_lo, FH * U + FH)]})

            pe.wait_ge(ones_ok, 1)
            group(GI["memK0"], {2: lambda: colsum("mem", MEM)})
            group(GI["memV0"])
            pe.wait_ge(ident_in, 16)
            group(GI["qm0"], {1: lambda: colsum("mix0", SEQ), 2: lambda: group_transposes(GI["memK0"]),
                              3: lambda: bcast("mix0", SEQ)})
            pe.wait_ge(g_ev, MT)
            for i in range(RT):
                c = BASE["xr"] + i
                fm_tile(bank[i % 2][:], c, c % RING, "mix0", KT, (xr_z, i - 1) if i >= 2 else None)
                if i == 1:
                    group_transposes(GI["qm0"])
                if 4 <= i < 4 + MH:
                    ma_values(i - 4)
                if 3 <= i < 3 + MH:
                    ma_transposes(i - 3)
                if 2 <= i < 2 + MH:
                    ma_scores(i - 2)
            pe.wait_ge(ma_lo, MH)
            for n, (kind, i) in enumerate(GY):
                c = BASE["gy"] + n
                if kind == "y":
                    fm_tile(bank[Y_BANK[i]][:], c, c % RING, "mix0", KT, Y_FREE[i])
                    continue
                pe.wait_ge(w_lo, c + 1)
                if i >= 3:
                    pe.wait_ge(gt_sig, i - 2)
                ks = gate_k(i)
                pe.wait_ge(xc_lo, ks[-1] + 1)
                for gate in range(2):
                    for m, k in enumerate(ks):
                        q = gate * len(ks) + m
                        mm = pass3(bank[2 + 3 * gate + i % 3][:], whi[:, c % RING, q * P:(q + 1) * P],
                                   wlo[:, c % RING, q * P:(q + 1) * P], mid_hi[:, k, :], mid_lo[:, k, :],
                                   m == 0, m == len(ks) - 1)
                mm.then_inc(w_used, 1)
            pe.wait_ge(gt_sig, RT)
            out_proj("out0", OUT0_ORDER, {MH + k: [(gt_lo, k + 1)] for k in range(RT)})
            ffn_up("up00")
            ffn_down("down00")
            ffn_up("up01")
            ffn_down("down01")
            group(GI["memK1"], {0: lambda: colsum("kv", SEQ)})
            group(GI["memV1"])
            group(GI["k"], {2: lambda: group_transposes(GI["memK1"])})
            group(GI["k'"], {1: lambda: group_transposes(GI["k"])})
            group(GI["v"], {1: lambda: group_transposes(GI["k'"])})
            group(GI["v'"])
            group(GI["q"])
            group(GI["q'"], {1: lambda: group_transposes(GI["q"])})
            group(GI["qm1"], {1: lambda: group_transposes(GI["q'"])})
            pe.wait_ge(g_ev, NB0[GI["q'"]] + TT)
            for s in range(len(HEADS) + 1):
                if s < len(HEADS):
                    at_scores(s)
                if s == 2:
                    group_transposes(GI["qm1"])
                    pe.wait_ge(g_ev, NB0[-1] + TT)
                    pe.wait_ge(v_ev, VB0[GI["v'"]] + TT)
                if 0 <= s - 2 < len(HEADS):
                    at_transposes(s - 2)
                if 0 <= s - 3 < len(HEADS):
                    at_values(s - 3)
            last = len(HEADS) - 1
            pe.wait_ge(at_e, TT * len(HEADS))
            out_proj("out1", list(range(FH)), {n: [(at_lo, n + 1)] for n in range(FH)},
                     {FH // 2: lambda: (at_transposes(last), at_values(last - 1)),
                      FH - 3: lambda: at_values(last)})
            ffn_up("up10")
            ffn_down("down10")
            ffn_up("up11")
            ffn_down("down11")

        @block.scalar
        def _(act):
            def split_hi(c, i=0, per=0):
                n = c + AHEAD
                act.wait_ge(raw_in[n % RAW], (16 * per // RAW) * i + 16 * (n // RAW + 1))
                if n >= RING:
                    act.wait_ge(w_used, per * i + (n - RING + 1))
                act.activation(whi[:, n % RING], raw[:, n % RAW], ACT.Copy).then_inc(w_hi, 1)

            def square(base, src, k, n, i=0, per=0):
                if base + k - 1 > 0 and not per:
                    act.wait_ge(sq_added, base + k - 1)
                act.activation(sq[:, k % 2, 0:n], src, ACT.Square).then_inc(sq_ready, 1)

            def stat_root(inst, n):
                S = ST[inst]
                act.wait_ge(st_cols, S + 1)
                if S > 0:
                    act.wait_ge(st_rc, S)
                act.activation(root[:, 0:n // P], SUM_BANK[inst][:, 0:n // P], ACT.Sqrt, bias=eps[:],
                               scale=1.0 / D).then_inc(st_root, 1)

            def stat_copy(inst):
                act.wait_ge(st_bcast, BC[inst] + 1)
                if inst == "ffn0":
                    act.wait_ge(yg_z, RT)
                if inst == "ffn1":
                    act.wait_ge(up_z, 2 * 2 * FH)
                act.activation(rb[:], BCAST_BANK[inst][:], ACT.Copy).then_inc(st_rb, 1)

            def high(inst, k, src, i=0, per=0):
                dh, _ = HDST[inst]
                g = COLS[GAIN[inst]] + k
                if per:
                    act.activation(dh[:, bass.ds(per * i + k, 1), :], src.unsqueeze(1), ACT.Copy,
                                   scale=cols[:, bass.ds(per * i + g, 1)]).then_inc(h_hi, 1)
                else:
                    act.activation(dh[:, k, :], src, ACT.Copy, scale=cols[:, g:g + 1]).then_inc(h_hi, 1)

            def group_squares(g):
                name, inp, T, hd = GROUPS[g]
                if not hd:
                    return
                r = rcol_mem if inp.startswith("mem") else rcol
                act.wait_ge(w_used, chunk_of(name, 3) + 1)
                if g < GI["memK1"]:
                    act.wait_ge(sq_added, 2 * KT)
                else:
                    act.wait_ge(sq_added, 4 * KT)
                act.wait_ge(st_rc, ST["mem" if name == "memK0" else "mix0" if g < GI["memK1"] else "kv"] + 1)
                for t in range(T if name == "qm1" else 0):
                    for h in range(MH):
                        ins = act.activation((sq[:, t, :] if t < 2 else rows(g, t))[:, h * hd:(h + 1) * hd],
                                             gset(g)[t][:, h * hd:(h + 1) * hd], ACT.Square,
                                             scale=r[:, t:t + 1], accum_out=gs[:, 0, t, h:h + 1])
                    ins.then_inc(g_ss, 1)
                for t in range(0 if name == "qm1" else T):
                    if NB0[g] + t >= 2:
                        act.wait_ge(g_ss, NB0[g] + t - 1)
                    act.activation(sq[:, t % 2], gset(g)[t][:], ACT.Square, scale=r[:, t:t + 1]).then_inc(g_sq, 1)
                act.wait_ge(g_ss, NB0[g] + T)
                if NB0[g] > 0:
                    act.wait_ge(g_kn, NB0[g])
                nh = 512 // hd
                act.activation(gs[:, 1, 0:T, 0:nh], gs[:, 0, 0:T, 0:nh], ACT.Sqrt, bias=eps[:],
                               scale=1.0 / hd).then_inc(g_rt, 1)

            def group_evac(g):
                name, _, T, hd = GROUPS[g]
                dst, f0, gain = {
                    "memK0": (kmT0, 0, col("g_km0")), "qm0": (qmT0, 0, col("g_qm0")),
                    "memK1": (kmT1, 0, col("g_km1")), "qm1": (qmT1, 0, col("g_qm1")),
                    "k": (kT, 0, col("g_ka")), "k'": (kT, 4, col("g_ka")),
                    "q": (qT, 0, gqs[:]), "q'": (qT, 4, gqs[:])}[name]
                for t in range(T):
                    act.wait_ge(g_tp, NB0[g] + t + 1)
                    act.activation(dst[:, f0:f0 + 4, t * P:(t + 1) * P],
                                   gset(g)[t][:].rearrange("p (f t) -> p f t", f=4), ACT.Copy,
                                   scale=gain).then_inc(g_ev, 1)

            def group_steps(name, after, evac):
                for j in range(4):
                    split_hi(chunk_of(name, j))
                    if j == 0 and after is not None:
                        group_squares(after)
                    if j == 2 and evac is not None:
                        group_evac(evac)

            def ma_exps(u):
                act.wait_ge(ma_nm, u + 1)
                if u > 0:
                    act.wait_ge(ma_t, u)
                    act.wait_ge(ma_rs, u)
                for t in range(TT):
                    act.activation(Pm0[:, t, :], bank[6 + t // 2][:, (t % 2) * MEM:(t % 2 + 1) * MEM], ACT.Exp,
                                   bias=nmx[:, 0, t:t + 1], scale=MHD ** -0.5,
                                   accum_out=mx[:, 0, 1, t:t + 1]).then_inc(ma_e, 1)

            def ma_high(u):
                act.wait_ge(ma_pv, u + 1)
                act.activation(mid_hi[:, RT + u, :], bank[2 + u % 2][:], ACT.Copy).then_inc(ma_hi, 1)

            def at_exps(s):
                kind, h = HEADS[s]
                act.wait_ge(at_nm, s + 1)
                if s >= 3:
                    act.wait_ge(at_t, s - 2)
                    act.wait_ge(at_rs, s - 2)
                at = 0
                for t in range(TT):
                    n = MEM if kind == "m" else P * (t + 1)
                    dst = Sc[:, s % 3, at:at + n]
                    act.activation(dst, bank[t][:, 0:n] if kind == "m" else dst, ACT.Exp,
                                   bias=nmx[:, s % 3, t:t + 1], scale=MHD ** -0.5 if kind == "m" else 1.0,
                                   accum_out=mx[:, s % 3, 1, t:t + 1]).then_inc(at_e, 1)
                    at += n

            def at_copy(s):
                act.wait_ge(at_t, s + 1)
                if s >= 1:
                    act.wait_ge(at_pv, s)
                act.activation(PTs[:, 0:512], bank[4][:], ACT.Copy).then_inc(at_pta, 1)

            def at_high(s):
                act.wait_ge(at_pv, s + 1)
                act.activation(mid_hi[:, OTILE[OUTPUTS.index(s)], :], bank[7][:], ACT.Copy).then_inc(at_hi, 1)

            def out_steps(name, inst, last=False):
                def body(i, stop=RING):
                    for m in range(2):
                        for half in range(2):
                            if 2 * m + half < stop:
                                split_hi(BASE[name] + 2 * m + half, i, RING)
                        if inst is not None:
                            act.wait_ge(o_add, 2 * i + (OI[name] + m + 1))
                            act.wait_ge(sq_added, 2 * i + (SQ[name] + m - 1))
                            high(inst, m, xT[:, 2 * i + m, :], i, 2)
                            square(SQ[name], xT[:, 2 * i + m, :], m, SEQ, i, 2)
                steps(act, KT // 2, body, False, (lambda i: body(i, RING - AHEAD)) if last else None)

            def up_steps(name):
                U = UI[name]
                L = name[2]
                q0 = FH * (U % 2)
                def body(i):
                    for p in range(2):
                        n = FH * U + p
                        if name[3] == "0" and isinstance(i, int) and p == 0:
                            stat_root("ffn" + L, SEQ)
                            stat_copy("ffn" + L)
                        for s in range(2):
                            split_hi(BASE[name] + 2 * p + s, i, RING)
                            act.wait_ge(up_z, RING * i + (2 * n + s + 1))
                            if not (name == "up00" and isinstance(i, int)):
                                act.wait_ge(up_lo, 2 * i + (n - 1))
                            f = COLS["ffn" + L] + 8 * (q0 + p) + 4 * s
                            act.activation(cf[:, 2 * s + p, :], zf[:, 2 * s + p, :], ACT.Identity,
                                           bias=cols[:, bass.ds(16 * i + (f + 3), 1)],
                                           scale=cols[:, bass.ds(16 * i + f, 1)]).then_inc(up_first, 1)
                        act.wait_ge(up_conv, RING * i + (2 * n + 2))
                        act.activation(cf[:, 2 + p, :], cf[:, 2 + p, :], ACT.Gelu_apprx_tanh).then_inc(up_gelu, 1)
                        act.wait_ge(up_hid, 2 * i + (n + 1))
                        act.activation(mid_hi[:, 2 * i + p, :], cf[:, p, :], ACT.Copy).then_inc(up_hi, 1)
                steps(act, FH // 2, body, name[3] == "0")

            act.wait_ge(ones_ok, 1)
            act.activation(lsc[:, 1, 0:1], eps[:], ACT.Square)
            act.wait_ge(cols_in, 16)
            split_hi(-3)
            for k in range(KT):
                if k % 4 == 0:
                    act.wait_ge(mem_in[k // 4], 16)
                high("mem0", k, memT[:, k, :])
                if k == 1:
                    split_hi(-2)
            for k in range(KT):
                square(0, memT[:, k, :], k, MEM)
                if k == 1:
                    split_hi(-1)
            split_hi(chunk_of("memK0", 0))
            for k in range(KT):
                if k % 4 == 0:
                    act.wait_ge(x_in[k // 4], 16)
                high("mix0", k, xT[:, k, :])
                if k in (2, 5):
                    split_hi(chunk_of("memK0", 1 + k // 3))
            square(KT, xT[:, 0, :], 0, SEQ)
            split_hi(chunk_of("memK0", 3))
            stat_root("mem", MEM)
            for k in range(1, KT):
                square(KT, xT[:, k, :], k, SEQ)
                if k in (2, 5):
                    split_hi(chunk_of("memV0", k // 3))
            split_hi(chunk_of("memV0", 2))
            group_squares(GI["memK0"])
            split_hi(chunk_of("memV0", 3))
            split_hi(chunk_of("qm0", 0))
            stat_root("mix0", SEQ)
            act.activation(lsc[:, 0, :], col_n("lam", RT), ACT.Abs).then_inc(lam_e, 1)
            act.wait_ge(lam_e, 1)
            act.activation(lsc[:, 1, :], lsc[:, 0, :], ACT.Exp, scale=-1.0).then_inc(lam_e, 1)
            split_hi(chunk_of("qm0", 1))
            group_evac(GI["memK0"])
            split_hi(chunk_of("qm0", 2))
            stat_copy("mix0")
            split_hi(chunk_of("qm0", 3))
            for i in range(RT):
                c = BASE["xr"] + i
                split_hi(c)
                if i == 0:
                    group_squares(GI["qm0"])
                if i == 2:
                    group_evac(GI["qm0"])
                act.wait_ge(xr_z, i + 1)
                act.activation(xc[:, i, :], tmp[:, i % 2, :], ACT.Identity, bias=col("conv_a", 5 * i + 4),
                               scale=col("conv_a", 5 * i + 3)).then_inc(xc_0, 1)
                if i >= 1:
                    conv_high(act, i - 1)
                if 4 <= i < 4 + MH:
                    ma_high(i - 4)
                if 2 <= i < 2 + MH:
                    ma_exps(i - 2)
            conv_high(act, RT - 1)

            def gelu_y(i):
                act.wait_ge(yg_z, i + 1)
                act.activation(gy[:, i, :], gy[:, i, :], ACT.Gelu_apprx_tanh).then_inc(yg_gelu, 1)

            chunks = iter(range(BASE["gy"], BASE["out0"]))

            def split_next():
                split_hi(next(chunks))

            act.wait_ge(lam_c, 1)
            for half in range(2):
                for t in range(BATCH):
                    m = BATCH * half + t
                    if half == 0 or t > 0:
                        split_next()
                        if half and t == 3:
                            split_next()
                    act.wait_ge(w_used, BASE["gy"] + GY.index(("g", m)) + 1)
                    if half:
                        act.wait_ge(gt_h, t + 1)
                    act.activation(R[:, t, :], bank[2 + m % 3][:], ACT.Sigmoid, bias=col("b_r", m))
                    act.activation(I[:, t, :], bank[5 + m % 3][:], ACT.Sigmoid, bias=col("b_i", m))\
                        .then_inc(gt_sig, 1)
                act.wait_ge(gt_sig, BATCH * (half + 1))
                for t in range(BATCH):
                    m = BATCH * half + t
                    act.activation(Aa[:, t, :], R[:, t, :], ACT.Exp, scale=lsc[:, 7, m:m + 1])\
                        .then_inc(gt_exp, 1)
                    act.wait_ge(gt_exp, 2 * m + 1)
                    act.activation(R[:, t, :], R[:, t, :], ACT.Tanh, scale=lsc[:, 7, m:m + 1])\
                        .then_inc(gt_exp, 1)
                    if t in (1, 3):
                        if not (half and t == 3):
                            split_next()
                for t in range(BATCH):
                    m = BATCH * half + t
                    act.wait_ge(gt_v, m + 1)
                    act.activation(R[:, t, :], R[:, t, :], ACT.Sqrt, scale=-1.0).then_inc(gt_root, 1)
                    if t == 0:
                        split_next()
                for i in range(2 * half, 2 * half + 2):
                    gelu_y(i)
            for i in range(4, RT):
                if i < RT - 1:
                    split_next()
                gelu_y(i)
            out_steps("out0", "ffn0")
            up_steps("up00")
            out_steps("down00", None)
            up_steps("up01")
            for k in range(KT):
                if k == 0:
                    act.wait_ge(mem_again, 16)
                high("mem1", k, memT[:, k, :])
            out_steps("down01", "kv")
            split_hi(chunk_of("memK1", 0))
            split_hi(chunk_of("memK1", 1))
            stat_root("kv", SEQ)
            split_hi(chunk_of("memK1", 2))
            act.wait_ge(w_used, BASE["memK1"])
            for k in range(KT):
                high("mix1", k, xT[:, k, :])
                if k == 2:
                    split_hi(chunk_of("memK1", 3))
                if k == 6:
                    split_hi(chunk_of("memV1", 0))
            for j in range(1, 4):
                split_hi(chunk_of("memV1", j))
                if j == 1:
                    group_squares(GI["memK1"])
            group_steps("k", None, None)
            group_evac(GI["memK1"])
            group_steps("k'", GI["k"], GI["k"])
            group_steps("v", GI["k'"], GI["k'"])
            group_steps("v'", None, None)
            group_steps("q", None, None)
            group_steps("q'", GI["q"], GI["q"])
            group_steps("qm1", GI["q'"], GI["q'"])
            group_squares(GI["qm1"])
            for s in range(len(HEADS) + 4):
                if 0 <= s - 3 < len(HEADS):
                    at_copy(s - 3)
                if s - 4 in OUTPUTS:
                    at_high(s - 4)
                if s == 1:
                    group_evac(GI["qm1"])
                if s < len(HEADS):
                    at_exps(s)
            out_steps("out1", "ffn1")
            up_steps("up10")
            out_steps("down10", None)
            up_steps("up11")
            out_steps("down11", None, last=True)

        @block.vector
        def _(dve):
            own = Tally(dve, dve_own)

            def add_square(base, k, n, i=0, per=0):
                dve.wait_ge(sq_ready, per * i + (base + k + 1))
                if base + k > 0:
                    dve.wait_ge(sq_added, per * i + (base + k))
                dve.tensor_tensor(ssum[:, 0:n], ssum[:, 0:n], sq[:, k % 2, 0:n], ALU.add).then_inc(sq_added, 1)

            def clear_sum(inst):
                if ST[inst] > 0:
                    dve.wait_ge(st_cols, ST[inst])
                own.link(dve.memset(ssum[:], 0.0))

            def stat(inst, n):
                S = ST[inst]
                r = rcol_mem if inst == "mem" else rcol
                dve.wait_ge(st_root, S + 1)
                if inst == "ffn0":
                    dve.wait_ge(g_sq, NB0[GI["memK1"]])
                if inst == "kv":
                    dve.wait_ge(g_kn, NB0[GI["memK1"]])
                if inst == "ffn1":
                    dve.wait_ge(g_ss, NB0[-1] + TT)
                dve.reciprocal(r[:, 0:n // P], root[:, 0:n // P]).then_inc(st_rc, 1)
                if inst not in BC:
                    return
                dve.wait_ge(st_rc, S + 1)
                if BC[inst] > 0:
                    dve.wait_ge(st_bcast, BC[inst])
                for t in range(n // P):
                    ins = dve.tensor_scalar(diag[:, t, :], ident[:], r[:, t:t + 1], None, ALU.mult)
                ins.then_inc(st_diag, 1)

            def low(inst, k, src, i=0, per=0):
                dh, dl = HDST[inst]
                g = COLS[GAIN[inst]] + k
                dve.wait_ge(h_hi, per * i + (KT * H[inst] + k + 1))
                if per:
                    at = bass.ds(per * i + k, 1)
                    dve.scalar_tensor_tensor(out=dl[:, at, :], in0=src, scalar=cols[:, bass.ds(per * i + g, 1)],
                                             in1=dh[:, at, :].bitcast(F32), op0=ALU.mult,
                                             op1=ALU.subtract).then_inc(h_lo, 1)
                else:
                    dve.scalar_tensor_tensor(out=dl[:, k, :], in0=src, scalar=cols[:, g:g + 1],
                                             in1=dh[:, k, :].bitcast(F32), op0=ALU.mult,
                                             op1=ALU.subtract).then_inc(h_lo, 1)

            def group_norm(g):
                name, inp, T, hd = GROUPS[g]
                nh = 512 // hd
                r = rcol_mem if inp.startswith("mem") else rcol
                for t in range(0 if name == "qm1" else T):
                    dve.wait_ge(g_sq, NB0[g] + t + 1)
                    if NI[g] > 0:
                        dve.wait_ge(g_rt, NI[g])
                    dve.tensor_reduce(gs[:, 0, t, 0:nh], sq[:, t % 2].rearrange("p (h d) -> p h d", h=nh),
                                      AX, ALU.add).then_inc(g_ss, 1)
                dve.wait_ge(g_rt, NI[g] + 1)
                if NB0[g] > 0:
                    dve.wait_ge(g_kn, NB0[g])
                own.link(dve.reciprocal(gs[:, 2, 0:T, 0:nh], gs[:, 1, 0:T, 0:nh]))
                own.link(dve.tensor_tensor(gs[:, 2, 0:T, 0:nh], gs[:, 2, 0:T, 0:nh],
                                           r[:, 0:T].unsqueeze(2).broadcast_to([P, T, nh]), ALU.mult))
                if NLAST[g] is not None and NLAST[g] != GI["qm0"]:
                    dve.wait_ge(g_tp, NB0[g])
                for t in range(T):
                    dve.tensor_tensor(rows(g, t).rearrange("p (h d) -> p h d", h=nh),
                                      gset(g)[t][:].rearrange("p (h d) -> p h d", h=nh),
                                      gs[:, 2, t, 0:nh].unsqueeze(2).broadcast_to([P, nh, hd]),
                                      ALU.mult).then_inc(g_kn, 1)

            def values_copy(g):
                name, inp, T, _ = GROUPS[g]
                r = rcol_mem if inp.startswith("mem") else rcol
                dve.wait_ge(w_used, chunk_of(name, 3) + 1)
                for t in range(T):
                    dst = {"memV0": Vm0[:, t % MT, :], "memV1": Vm1[:, t % MT, :],
                           "v": V[:, t, 0:512], "v'": V[:, t, 512:1024]}[name]
                    dve.tensor_scalar(dst, gset(g)[t][:], r[:, t:t + 1], None, ALU.mult).then_inc(v_ev, 1)

            def conv_xr(i):
                dve.wait_ge(w_used, BASE["xr"] + i + 1)
                if i == 0:
                    dve.wait_ge(st_rb, BC["mix0"] + 1)
                else:
                    dve.wait_ge(xc_done, i)
                dve.tensor_tensor(tmp[:, i % 2, :], bank[i % 2][:], rb[:], ALU.mult).then_inc(xr_z, 1)
                dve.wait_ge(xr_z, i + 1)
                dve.wait_ge(xc_0, i + 1)
                for n, tap in enumerate((2, 1, 0)):
                    sh = 3 - tap
                    ins = dve.scalar_tensor_tensor(out=xc[:, i, sh:SEQ], in0=tmp[:, i % 2, 0:SEQ - sh],
                                                   scalar=col("conv_a", 5 * i + tap), in1=xc[:, i, sh:SEQ],
                                                   op0=ALU.mult, op1=ALU.add)
                    if tap:
                        own.link(ins)
                    else:
                        ins.then_inc(xc_done, 1)

            def conv_low(i):
                dve.wait_ge(xc_hi, i + 1)
                dve.wait_ge(xc_done, i + 1)
                dve.tensor_tensor(mid_lo[:, i, :], xc[:, i, :], mid_hi[:, i, :].bitcast(F32), ALU.subtract)\
                    .then_inc(xc_lo, 1)

            def ma_max(u):
                for half in range(2):
                    dve.wait_ge(ma_s, 2 * u + half + 1)
                    if u > 0:
                        dve.wait_ge(ma_e, TT * u)
                    own.inc(dve.tensor_reduce(mx[:, 0, 0, 2 * half:2 * half + 2],
                                              bank[6 + half][:].rearrange("p (t m) -> p t m", t=2), AX, ALU.max))
                own.wait()
                dve.tensor_scalar(nmx[:, 0, :], mx[:, 0, 0, :], -MHD ** -0.5, None, ALU.mult).then_inc(ma_nm, 1)

            def ma_scale(u):
                dve.wait_ge(ma_e, TT * (u + 1))
                if u > 0:
                    dve.wait_ge(ma_p, u)
                dve.reciprocal(mx[:, 0, 2, :], mx[:, 0, 1, :]).then_inc(ma_rs, 1)
                dve.wait_ge(ma_rs, u + 1)
                for t in range(TT):
                    ins = dve.tensor_scalar(Pm0[:, t, :], Pm0[:, t, :], mx[:, 0, 2, t:t + 1], None, ALU.mult)
                ins.then_inc(ma_p, 1)

            def ma_copy(u):
                dve.wait_ge(ma_t, u + 1)
                if u > 0:
                    dve.wait_ge(ma_pv, u)
                for m in range(MT):
                    ins = dve.tensor_copy(PTm0[:, m, :], bank[4 + m][:])
                ins.then_inc(ma_pt, 1)

            def ma_low(u):
                k = RT + u
                dve.wait_ge(ma_hi, u + 1)
                dve.tensor_tensor(mid_lo[:, k, :], bank[2 + u % 2][:], mid_hi[:, k, :].bitcast(F32),
                                  ALU.subtract).then_inc(ma_lo, 1)

            def at_max(s):
                kind, h = HEADS[s]
                if kind == "c":
                    dve.wait_ge(strip_in[h % 2], 16 * (h // 2 + 1))
                if s >= 3:
                    dve.wait_ge(at_t, s - 2)
                    dve.wait_ge(at_e, TT * (s - 2))
                at = 0
                for t in range(TT):
                    dve.wait_ge(at_s, TT * s + t + 1)
                    m = mx[:, s % 3, 0, t:t + 1]
                    if kind == "m":
                        dve.tensor_reduce(m, bank[t][:, 0:MEM], AX, ALU.max).then_inc(at_add, 1)
                    else:
                        n = P * (t + 1)
                        dve.tensor_tensor_reduce(Sc[:, s % 3, at:at + n], bank[t][:, 0:n],
                                                 strip[:, h % 2, SEQ - n:SEQ], 1.0, -3.0e38, ALU.add, ALU.max,
                                                 m).then_inc(at_add, 1)
                        at += n
                dve.wait_ge(at_add, TT * (s + 1))
                dve.tensor_scalar(nmx[:, s % 3, :], mx[:, s % 3, 0, :], -MHD ** -0.5 if kind == "m" else -1.0,
                                  None, ALU.mult).then_inc(at_nm, 1)

            def at_reciprocal(s):
                dve.wait_ge(at_e, TT * (s + 1))
                if s >= 3:
                    dve.wait_ge(at_p, s - 2)
                dve.reciprocal(mx[:, s % 3, 2, :], mx[:, s % 3, 1, :]).then_inc(at_rs, 1)

            def at_copy(s):
                dve.wait_ge(at_t, s + 1)
                if s > 0:
                    dve.wait_ge(at_pv, s)
                ins = dve.tensor_copy(PTs[:, 512:1024], bank[5][:])
                if HEADS[s][0] == "c":
                    ins = dve.tensor_copy(PTs[:, 1024:1280], bank[6][:, 0:256])
                ins.then_inc(at_ptd, 1)

            def at_low(s):
                n = OUTPUTS.index(s)
                k = OTILE[n]
                dve.wait_ge(at_hi, n + 1)
                dve.tensor_tensor(mid_lo[:, k, :], bank[7][:], mid_hi[:, k, :].bitcast(F32), ALU.subtract)\
                    .then_inc(at_lo, 1)

            def out_steps(name, inst):
                with dve.Fori(0, KT // 2) as i:
                    for m in range(2):
                        dve.wait_ge(w_used, RING * i + (BASE[name] + 2 * m + 2))
                        dve.tensor_tensor(xT[:, bass.ds(2 * i + m, 1), :], xT[:, bass.ds(2 * i + m, 1), :],
                                          bank[OUT_BANK[name] + m][:].unsqueeze(1), ALU.add).then_inc(o_add, 1)
                        if inst is not None:
                            dve.wait_ge(o_add, 2 * i + (OI[name] + m + 1))
                            low(inst, m, xT[:, bass.ds(2 * i + m, 1), :], i, 2)
                            add_square(SQ[name], m, SEQ, i, 2)

            def up_steps(name):
                U = UI[name]
                L = name[2]
                q0 = FH * (U % 2)

                def body(i):
                    for p in range(2):
                        n = FH * U + p
                        if name[3] == "0" and isinstance(i, int) and p == 0:
                            stat("ffn" + L, SEQ)
                            dve.wait_ge(st_rb, BC["ffn" + L] + 1)
                        for s in range(2):
                            dve.wait_ge(w_used, RING * i + (BASE[name] + 2 * p + s + 1))
                            if not (name == "up00" and isinstance(i, int)):
                                dve.wait_ge(up_conv, RING * i + (2 * n + s - 3))
                            dve.tensor_tensor(zf[:, 2 * s + p, :], bank[2 * s + p][:], rb[:], ALU.mult)\
                                .then_inc(up_z, 1)
                        for s in range(2):
                            z, acc = zf[:, 2 * s + p, :], cf[:, 2 * s + p, :]
                            f = COLS["ffn" + L] + 8 * (q0 + p) + 4 * s
                            dve.wait_ge(up_z, RING * i + (2 * n + s + 1))
                            dve.wait_ge(up_first, RING * i + (2 * n + s + 1))
                            dve.scalar_tensor_tensor(
                                out=acc[:, 1:SEQ], in0=z[:, 0:SEQ - 1],
                                scalar=cols[:, bass.ds(16 * i + (f + 1), 1)], in1=acc[:, 1:SEQ],
                                op0=ALU.mult, op1=ALU.add).then_inc(up_tap, 1)
                            dve.wait_ge(up_tap, RING * i + (2 * n + s + 1))
                            dve.scalar_tensor_tensor(
                                out=acc[:, 2:SEQ], in0=z[:, 0:SEQ - 2],
                                scalar=cols[:, bass.ds(16 * i + (f + 2), 1)], in1=acc[:, 2:SEQ],
                                op0=ALU.mult, op1=ALU.add).then_inc(up_conv, 1)
                        dve.wait_ge(up_gelu, 2 * i + (n + 1))
                        dve.wait_ge(up_conv, RING * i + (2 * n + 2))
                        dve.tensor_tensor(cf[:, p, :], cf[:, p, :], cf[:, 2 + p, :], ALU.mult).then_inc(up_hid, 1)
                        dve.wait_ge(up_hid, 2 * i + (n + 1))
                        dve.wait_ge(up_hi, 2 * i + (n + 1))
                        dve.tensor_tensor(mid_lo[:, bass.ds(2 * i + p, 1), :], cf[:, p, :].unsqueeze(1),
                                          mid_hi[:, bass.ds(2 * i + p, 1), :].bitcast(F32), ALU.subtract)\
                            .then_inc(up_lo, 1)
                steps(dve, FH // 2, body, name[3] == "0")

            def log_sigmoid():
                e, t, y, z, p, r = (lsc[:, n, :] for n in (1, 2, 3, 4, 5, 6))
                dve.wait_ge(lam_e, 2)
                own.link(dve.tensor_scalar(t, e, 2.0, None, ALU.add))
                own.link(dve.reciprocal(r, t))
                own.link(dve.tensor_tensor(y, e, r, ALU.mult))
                own.link(dve.tensor_tensor(z, y, y, ALU.mult))
                own.link(dve.tensor_scalar(p, z, 1.0 / 17, 1.0 / 15, ALU.mult, ALU.add))
                for n in range(13, 0, -2):
                    own.link(dve.tensor_tensor(p, p, z, ALU.mult))
                    own.link(dve.tensor_scalar(p, p, 1.0 / n, None, ALU.add))
                own.link(dve.tensor_tensor(p, p, y, ALU.mult))
                own.link(dve.tensor_scalar(p, p, 2.0 * RG_C, None, ALU.mult))
                own.link(dve.tensor_scalar(t, col_n("lam", RT), 0.0, RG_C, ALU.min, ALU.mult))
                dve.tensor_tensor(lsc[:, 7, :], t, p, ALU.subtract).then_inc(lam_c, 1)

            dve.memset(eps[:], EPS)
            dve.memset(ones[:], 1.0).then_inc(ones_ok, 1)
            clear_sum("mem")
            dve.wait_ge(w_hi, 1)
            dve.tensor_tensor(wlo[:, 0], raw[:, 0], whi[:, 0].bitcast(F32), ALU.subtract).then_inc(w_lo, 1)
            dve.wait_ge(cols_in, 16)
            for k in range(KT):
                low("mem0", k, memT[:, k, :])
            for k in range(KT):
                add_square(0, k, MEM)
            for k in range(KT):
                low("mix0", k, xT[:, k, :])
            clear_sum("mix0")
            stat("mem", MEM)
            for k in range(KT):
                add_square(KT, k, SEQ)
            values_copy(GI["memV0"])
            group_norm(GI["memK0"])
            dve.wait_ge(ident_in, 16)
            stat("mix0", SEQ)
            dve.tensor_scalar(gqs[:], col("g_qa"), AHD ** -0.5, None, ALU.mult).then_inc(gq_ok, 1)
            log_sigmoid()
            group_norm(GI["qm0"])
            for i in range(RT):
                conv_xr(i)
                if i >= 1:
                    conv_low(i - 1)
                if 4 <= i < 4 + MH:
                    ma_low(i - 4)
                if 3 <= i < 3 + MH:
                    ma_copy(i - 3)
                if 2 <= i < 2 + MH:
                    ma_max(i - 2)
                    ma_scale(i - 2)
            conv_low(RT - 1)

            def rms_y(i):
                n = GY.index(("y", i))
                dve.wait_ge(w_used, BASE["gy"] + n + 1)
                dve.tensor_tensor(gy[:, i, :], bank[Y_BANK[i]][:], rb[:], ALU.mult).then_inc(yg_z, 1)

            def main(m):
                dve.wait_ge(yg_gelu, m + 1)
                dve.wait_ge(gt_h, m + 1)
                g = max(g for g in range(RT) if m in gate_k(g))
                dve.wait_ge(w_used, BASE["gy"] + GY.index(("g", g)) + 1)
                own.link(dve.tensor_tensor(xc[:, m, :], xc[:, m, :], gy[:, m, :], ALU.mult))
                own.link(dve.tensor_copy(mid_hi[:, m, :], xc[:, m, :]))
                dve.tensor_tensor(mid_lo[:, m, :], xc[:, m, :], mid_hi[:, m, :].bitcast(F32), ALU.subtract)\
                    .then_inc(gt_lo, 1)

            for half in range(2):
                for t in range(BATCH):
                    m = BATCH * half + t
                    if half and t >= 3:
                        main(t - 3)
                    dve.wait_ge(gt_sig, m + 1)
                    dve.tensor_tensor(I[:, t, :], I[:, t, :], xc[:, m, :], ALU.mult).then_inc(gt_ix, 1)
                for t in range(BATCH):
                    m = BATCH * half + t
                    if t == 2 * (1 - half):
                        rms_y(2 * half)
                    dve.wait_ge(gt_exp, 2 * m + 2)
                    if m > 0:
                        dve.wait_ge(gt_v, m)
                    own.link(dve.tensor_tensor(a2, Aa[:, t, :], Aa[:, t, :], ALU.mult))
                    dve.scalar_tensor_tensor(out=R[:, t, :], in0=a2, scalar=1.0, in1=R[:, t, :],
                                             op0=ALU.add, op1=ALU.mult).then_inc(gt_v, 1)
                rms_y(2 * half + 1)
                for t in range(BATCH):
                    m = BATCH * half + t
                    dve.wait_ge(gt_root, m + 1)
                    dve.wait_ge(gt_ix, m + 1)
                    own.link(dve.tensor_tensor(I[:, t, :], I[:, t, :], R[:, t, :], ALU.mult))
                    dve.tensor_tensor_scan(xc[:, m, :], Aa[:, t, :], I[:, t, :], 0.0, ALU.mult, ALU.add)\
                        .then_inc(gt_h, 1)
            done = 2
            for i in range(4, RT):
                rms_y(i)
                for m in range(done, min(i, done + 2)):
                    main(m)
                    done += 1
            while done < RT:
                main(done)
                done += 1
            clear_sum("ffn0")
            out_steps("out0", "ffn0")
            up_steps("up00")
            out_steps("down00", None)
            up_steps("up01")
            for k in range(KT):
                low("mem1", k, memT[:, k, :])
            clear_sum("kv")
            out_steps("down01", "kv")
            stat("kv", SEQ)
            for k in range(KT):
                low("mix1", k, xT[:, k, :])
            group_norm(GI["memK1"])
            values_copy(GI["memV1"])
            group_norm(GI["k"])
            group_norm(GI["k'"])
            values_copy(GI["v"])
            values_copy(GI["v'"])
            group_norm(GI["q"])
            group_norm(GI["q'"])
            for s in range(len(HEADS) + 4):
                if 0 <= s - 3 < len(HEADS):
                    at_copy(s - 3)
                if s - 4 in OUTPUTS:
                    at_low(s - 4)
                if s < len(HEADS):
                    at_max(s)
                if s == 1:
                    group_norm(GI["qm1"])
                if 0 <= s - 1 < len(HEADS):
                    at_reciprocal(s - 1)
            clear_sum("ffn1")
            out_steps("out1", "ffn1")
            up_steps("up10")
            out_steps("down10", None)
            up_steps("up11")
            out_steps("down11", None)


def _feature_rows(a, n):
    import numpy as np
    return np.ascontiguousarray(a.reshape(a.shape[0], n, P).transpose(2, 1, 0))


def _stationary(w, order=None, chunks=1):
    import numpy as np
    K, M = w.shape
    w = w.reshape(K // P, P, M // P, P)
    if order is not None:
        w = w[order]
    w = w.transpose(2, 1, 0, 3)
    w = w.reshape(M // P, P, chunks, K // chunks).transpose(0, 2, 1, 3)
    return np.ascontiguousarray(w.reshape(M // P * chunks, P, K // chunks))


def _moving(w):
    import numpy as np
    G = w.shape[1] // 512
    w = w.reshape(4, 2, P, G, 512).transpose(3, 0, 2, 1, 4)
    return np.ascontiguousarray(w.reshape(G * 4, P, 1024))


def _gates(w_r, w_i):
    import numpy as np
    dense = np.zeros((2, D_RNN, D_RNN), np.float32)
    for g, w in enumerate((w_r, w_i)):
        for b in range(D_RNN // RGB):
            dense[g, b * RGB:(b + 1) * RGB, b * RGB:(b + 1) * RGB] = w[b]
    out = np.zeros((RT, P, 8 * P), np.float32)
    for m in range(RT):
        ks = gate_k(m)
        for g in range(2):
            for n, k in enumerate(ks):
                q = g * len(ks) + n
                out[m, :, q * P:(q + 1) * P] = dense[g, k * P:(k + 1) * P, m * P:(m + 1) * P]
    return out


def _strips(rel_bias):
    import numpy as np
    p, w = np.arange(P)[:, None], np.arange(SEQ)[None, :]
    rel = np.clip(p - (w - (SEQ - P)), -63, 256) + 63
    s = rel_bias[:, rel]
    s[:, 0:64, SEQ - 64:SEQ] = MASKED
    return np.ascontiguousarray(s)


def _columns(d):
    import numpy as np
    col = lambda v: v.reshape(-1, P).T
    parts = {"conv_a": np.stack([*(col(d["w_conv_a"][0, t]) for t in range(4)), col(d["b_conv_a"][0])], 2)
             .reshape(P, 5 * RT), "b_r": col(d["b_r_a"][0]), "b_i": col(d["b_i_a"][0]), "lam": col(d["lam_a"][0]),
             "g_kv": col(d["g_kv"]), "g_qa": np.tile(d["g_q_att"][0], 2)[:, None],
             "g_ka": np.tile(d["g_k_att"], 2)[:, None]}
    for L in range(2):
        parts["g_mix%d" % L] = col(d["g_mix"][L])
        parts["g_mem%d" % L] = col(d["g_mem"][L])
        parts["g_ffn%d" % L] = col(d["g_ffn"][L])
        parts["g_qm%d" % L] = d["g_q_mem"][L][:, None]
        parts["g_km%d" % L] = d["g_k_mem"][L][:, None]
        w, b = d["w_dw_ffn"][L], d["b_dw_ffn"][L]
        taps = [col(w[2]), col(w[1]), col(w[0]), col(b)]
        both = [t[:, s * FT:(s + 1) * FT] for s in range(2) for t in taps]
        parts["ffn%d" % L] = np.stack(both, 2).reshape(P, 8 * FT)
    out = np.zeros((P, NCOLS), np.float32)
    for name, at in COLS.items():
        out[:, at:at + parts[name].shape[1]] = parts[name]
    return out


def kernel(**inputs):
    import numpy as np
    import concourse.bacc as bacc
    from concourse.bass_utils import run_bass_kernel_spmd

    d = {k: np.asarray(v) for k, v in inputs.items()}
    arrays = {"xT": _feature_rows(d["x"][0], KT), "memT": _feature_rows(d["mem"][0], KT),
              "cols": _columns(d), "ident": np.eye(P, dtype=np.float32), "strips": _strips(d["rel_bias_b"][0])}
    w = d["w_in_a"][0]
    arrays["w_xr"] = _stationary(w[:, 0:D_RNN])
    arrays["w_qm0"] = _moving(w[:, 2 * D_RNN:])
    tiles = {"g": _gates(d["w_r_a"][0], d["w_i_a"][0]), "y": _stationary(w[:, D_RNN:2 * D_RNN])}
    arrays["w_gy"] = np.stack([tiles[kind][i] for kind, i in GY])
    arrays["w_out0"] = _stationary(d["w_out_a"][0], OUT0_ORDER, 2)
    arrays["w_out1"] = _stationary(d["w_out_b"][0], None, 2)
    arrays["w_k"] = _moving(d["w_kv"][:, 0:D])
    arrays["w_v"] = _moving(d["w_kv"][:, D:])
    arrays["w_q"] = _moving(d["w_in_b"][0][:, 0:D])
    arrays["w_qm1"] = _moving(d["w_in_b"][0][:, D:])
    for L in range(2):
        arrays["w_memK%d" % L] = _moving(d["w_mem_kv"][L][:, 0:512])
        arrays["w_memV%d" % L] = _moving(d["w_mem_kv"][L][:, 512:])
        up = _stationary(d["w_up"][L])
        for f in range(2):
            pairs = [t for p in range(FH) for t in (FH * f + p, FT + FH * f + p)]
            arrays["w_up%d%d" % (L, f)] = np.ascontiguousarray(up[pairs])
            rows = d["w_down"][L][FH * f * P:FH * (f + 1) * P]
            arrays["w_down%d%d" % (L, f)] = _stationary(rows, None, 2)
    nc = bacc.Bacc("TRN2", target_bir_lowering=False, num_devices=1, dynamic_dma_scratch_size=1024)
    A = {n: nc.dram_tensor("in_" + n, a.shape, F32, kind="ExternalInput").ap() for n, a in arrays.items()}
    out = nc.dram_tensor("out", (P, KT, SEQ), F32, kind="ExternalOutput").ap()
    build(nc, A, out)
    r = run_bass_kernel_spmd(nc, [{"in_" + n: a for n, a in arrays.items()}], core_ids=[0])
    y = np.asarray(r.results[0]["out"])
    return np.ascontiguousarray(y.transpose(2, 1, 0).reshape(1, SEQ, D))
```
